# Optimizing a Trainium2 kernel written in Bass

```python
import jax
import jax.numpy as jnp
from jax import lax
import numpy as np

D_MODEL = 1024
BATCH = 1
SEQ = 2048
DEPTH = 1

N_MIXERS = 4
N_HEADS = 16
HEAD_DIM = D_MODEL // N_HEADS
D_FF = ((8 * D_MODEL // 3 + 127) // 128) * 128
SHORT_CONV_K = 3
CONFORMER_K = 31
FFN_CONV_K = 3
FOX_Q_BLOCK = 128
MOBA_BLOCK = 256
MOBA_TOPK = 3
MOBA_Q_CHUNK = 64
ALIBI_MAX_EXP = 8.0
RMS_EPS = 1e-6
LN_EPS = 1e-5
NEG_INF = -1e30

kernel_name = 'hybrid_interleaved_conv_fox_moba_block'

def rmsnorm(x, g):
    xf = x.astype(jnp.float32)
    y = xf * lax.rsqrt(jnp.mean(xf * xf, axis=-1, keepdims=True) + RMS_EPS)
    return (y * g.astype(jnp.float32)).astype(x.dtype)

def layernorm(x, g, b):
    xf = x.astype(jnp.float32)
    xc = xf - jnp.mean(xf, axis=-1, keepdims=True)
    y = xc * lax.rsqrt(jnp.mean(xc * xc, axis=-1, keepdims=True) + LN_EPS)
    return (y * g.astype(jnp.float32) + b.astype(jnp.float32)).astype(x.dtype)

def causal_dwconv(x, w):
    k = w.shape[0]
    return lax.conv_general_dilated(
        x, w[:, None, :].astype(x.dtype), window_strides=(1,), padding=[(k - 1, 0)],
        dimension_numbers=('NWC', 'WIO', 'NWC'), feature_group_count=x.shape[-1])

def to_heads(t):
    b, s, _ = t.shape
    return t.reshape(b, s, N_HEADS, HEAD_DIM).transpose(0, 2, 1, 3)

def from_head_blocks(o):
    n, b, h, blk, dh = o.shape
    return o.transpose(1, 0, 3, 2, 4).reshape(b, n * blk, h * dh)

def alibi_slopes():
    return jnp.exp2(-ALIBI_MAX_EXP * jnp.arange(1, N_HEADS + 1, dtype=jnp.float32) / N_HEADS)

def short_conv_mixer(h, w_in, w_conv, w_out):
    b_gate, c_gate, xh = jnp.split(h @ w_in, 3, axis=-1)
    return (b_gate * causal_dwconv(c_gate * xh, w_conv)) @ w_out

def conformer_conv_mixer(h, w_in, w_dw, b_dw, ln_g, ln_b, w_out):
    a, g = jnp.split(h @ w_in, 2, axis=-1)
    u = causal_dwconv(a * jax.nn.sigmoid(g), w_dw) + b_dw
    return jax.nn.silu(layernorm(u, ln_g, ln_b)) @ w_out

def fox_attention(h, w_in, b_f, g_q, g_k, w_out):
    b, s, d = h.shape
    q, k, v, f_logit = jnp.split(h @ w_in, [d, 2 * d, 3 * d], axis=-1)
    q = rmsnorm(to_heads(q), g_q)
    k = rmsnorm(to_heads(k), g_k)
    v = to_heads(v)
    log_f = jax.nn.log_sigmoid((f_logit + b_f).astype(jnp.float32))
    cum_f = jnp.cumsum(log_f, axis=1).transpose(0, 2, 1)
    n_blk = s // FOX_Q_BLOCK
    q_blk = q.reshape(b, N_HEADS, n_blk, FOX_Q_BLOCK, HEAD_DIM).transpose(2, 0, 1, 3, 4)
    f_blk = cum_f.reshape(b, N_HEADS, n_blk, FOX_Q_BLOCK).transpose(2, 0, 1, 3)
    k_pos = jnp.arange(s)
    scale = HEAD_DIM ** -0.5

    def block(args):
        q_i, f_i, i = args
        q_pos = i * FOX_Q_BLOCK + jnp.arange(FOX_Q_BLOCK)
        logits = jnp.einsum('bhqd,bhkd->bhqk', q_i, k, preferred_element_type=jnp.float32) * scale
        logits = jnp.where(k_pos[None, :] <= q_pos[:, None],
                           logits + (f_i[..., :, None] - cum_f[:, :, None, :]), NEG_INF)
        p = jax.nn.softmax(logits, axis=-1)
        return jnp.einsum('bhqk,bhkd->bhqd', p.astype(v.dtype), v)

    o = lax.map(block, (q_blk, f_blk, jnp.arange(n_blk)))
    return from_head_blocks(o) @ w_out

def moba_attention(h, w_in, g_q, g_k, w_out):
    b, s, d = h.shape
    q, k, v = jnp.split(h @ w_in, 3, axis=-1)
    q = rmsnorm(to_heads(q), g_q)
    k = rmsnorm(to_heads(k), g_k)
    v = to_heads(v)
    n_kb = -(-s // MOBA_BLOCK)
    pad = ((0, 0), (0, 0), (0, n_kb * MOBA_BLOCK - s), (0, 0))
    kp = jnp.pad(k, pad)
    vp = jnp.pad(v, pad)
    k_blocks = kp.reshape(b, N_HEADS, n_kb, MOBA_BLOCK, HEAD_DIM)
    k_mean = jnp.mean(k_blocks.astype(jnp.float32), axis=3)
    kb_flat = k_blocks.reshape(b * N_HEADS, n_kb, MOBA_BLOCK, HEAD_DIM)
    vb_flat = vp.reshape(b * N_HEADS, n_kb, MOBA_BLOCK, HEAD_DIM)
    top_k = min(MOBA_TOPK, n_kb)
    slopes = alibi_slopes()[None, :, None, None]
    blk_ids = jnp.arange(n_kb)
    offs = jnp.arange(MOBA_BLOCK)
    scale = HEAD_DIM ** -0.5
    gather = jax.vmap(lambda blocks, ids: blocks[ids])

    def chunk(ci):
        q0 = ci * MOBA_Q_CHUNK
        own = q0 // MOBA_BLOCK
        q_pos = q0 + jnp.arange(MOBA_Q_CHUNK)
        qc = lax.dynamic_slice_in_dim(q, q0, MOBA_Q_CHUNK, axis=2)
        gate = jnp.einsum('bhqd,bhnd->bhqn', qc.astype(jnp.float32), k_mean)
        gate = jnp.where(blk_ids < own, gate, NEG_INF)
        _, sel = lax.top_k(gate, top_k)
        valid = sel < own
        ids = sel.reshape(b * N_HEADS, MOBA_Q_CHUNK * top_k)
        k_sel = gather(kb_flat, ids).reshape(b, N_HEADS, MOBA_Q_CHUNK, top_k, MOBA_BLOCK, HEAD_DIM)
        v_sel = gather(vb_flat, ids).reshape(b, N_HEADS, MOBA_Q_CHUNK, top_k, MOBA_BLOCK, HEAD_DIM)
        pos_sel = sel[..., None] * MOBA_BLOCK + offs
        s_sel = jnp.einsum('bhqd,bhqjkd->bhqjk', qc, k_sel, preferred_element_type=jnp.float32) * scale
        s_sel = s_sel - slopes[..., None] * (q_pos[:, None, None] - pos_sel).astype(jnp.float32)
        s_sel = jnp.where(valid[..., None], s_sel, NEG_INF).reshape(b, N_HEADS, MOBA_Q_CHUNK, top_k * MOBA_BLOCK)
        k_own = lax.dynamic_slice_in_dim(kp, own * MOBA_BLOCK, MOBA_BLOCK, axis=2)
        v_own = lax.dynamic_slice_in_dim(vp, own * MOBA_BLOCK, MOBA_BLOCK, axis=2)
        own_pos = own * MOBA_BLOCK + offs
        s_own = jnp.einsum('bhqd,bhkd->bhqk', qc, k_own, preferred_element_type=jnp.float32) * scale
        s_own = jnp.where(own_pos[None, :] <= q_pos[:, None],
                          s_own - slopes * (q_pos[:, None] - own_pos[None, :]).astype(jnp.float32), NEG_INF)
        p = jax.nn.softmax(jnp.concatenate([s_sel, s_own], axis=-1), axis=-1).astype(v.dtype)
        p_sel = p[..., :top_k * MOBA_BLOCK].reshape(b, N_HEADS, MOBA_Q_CHUNK, top_k, MOBA_BLOCK)
        p_own = p[..., top_k * MOBA_BLOCK:]
        return (jnp.einsum('bhqjk,bhqjkd->bhqd', p_sel, v_sel)
                + jnp.einsum('bhqk,bhkd->bhqd', p_own, v_own))

    o = lax.map(chunk, jnp.arange(s // MOBA_Q_CHUNK))
    return from_head_blocks(o) @ w_out

def conv_ffn(h, w_up, w_conv, w_down):
    u, g = jnp.split(h @ w_up, 2, axis=-1)
    return (jax.nn.silu(causal_dwconv(u, w_conv)) * g) @ w_down

def setup_inputs(seed: int = 0) -> dict:
    key = jax.random.key(seed)
    ks = iter(jax.random.split(key, 40))
    f32 = jnp.float32
    D = D_MODEL

    def w(shape, fan_in, mult=1.0):
        return jax.random.normal(next(ks), shape, f32) * (mult * fan_in ** -0.5)

    def gain(shape):
        return 1.0 + 0.02 * jax.random.normal(next(ks), shape, f32)

    def bias(shape):
        return 0.02 * jax.random.normal(next(ks), shape, f32)

    n_a, n_b, n_c, n_d = [len(range(m, DEPTH, N_MIXERS)) for m in range(N_MIXERS)]
    return {
        'x': jax.random.normal(next(ks), (BATCH, SEQ, D), f32),
        'c': jax.random.normal(next(ks), (BATCH, D), f32),
        'ln_mix_g': gain((DEPTH, D)),
        'ln_ffn_g': gain((DEPTH, D)),
        'ada_w': w((DEPTH, D, 6 * D), D, 0.5),
        'ada_b': bias((DEPTH, 6 * D)),
        'ffn_up': w((DEPTH, D, 2 * D_FF), D),
        'ffn_conv': w((DEPTH, FFN_CONV_K, D_FF), FFN_CONV_K),
        'ffn_down': w((DEPTH, D_FF, D), D_FF),
        'sc_in': w((n_a, D, 3 * D), D),
        'sc_conv': w((n_a, SHORT_CONV_K, D), SHORT_CONV_K),
        'sc_out': w((n_a, D, D), D),
        'cf_in': w((n_b, D, 2 * D), D),
        'cf_dw': w((n_b, CONFORMER_K, D), CONFORMER_K),
        'cf_dw_b': bias((n_b, D)),
        'cf_ln_g': gain((n_b, D)),
        'cf_ln_b': bias((n_b, D)),
        'cf_out': w((n_b, D, D), D),
        'fox_in': w((n_c, D, 3 * D + N_HEADS), D),
        'fox_bf': jax.random.uniform(next(ks), (n_c, N_HEADS), f32, 1.0, 4.0),
        'fox_qn': gain((n_c, HEAD_DIM)),
        'fox_kn': gain((n_c, HEAD_DIM)),
        'fox_out': w((n_c, D, D), D),
        'moba_in': w((n_d, D, 3 * D), D),
        'moba_qn': gain((n_d, HEAD_DIM)),
        'moba_kn': gain((n_d, HEAD_DIM)),
        'moba_out': w((n_d, D, D), D),
    }

def reference(x, c, ln_mix_g, ln_ffn_g, ada_w, ada_b, ffn_up, ffn_conv, ffn_down,
              sc_in, sc_conv, sc_out, cf_in, cf_dw, cf_dw_b, cf_ln_g, cf_ln_b, cf_out,
              fox_in, fox_bf, fox_qn, fox_kn, fox_out, moba_in, moba_qn, moba_kn, moba_out):
    cond = jax.nn.silu(c)
    for i in range(DEPTH):
        kind = i % N_MIXERS
        j = i // N_MIXERS
        mod = cond @ ada_w[i] + ada_b[i]
        sh1, sc1, gt1, sh2, sc2, gt2 = [m[:, None, :] for m in jnp.split(mod, 6, axis=-1)]
        h = rmsnorm(x, ln_mix_g[i]) * (1.0 + sc1) + sh1
        if kind == 0:
            y = short_conv_mixer(h, sc_in[j], sc_conv[j], sc_out[j])
        elif kind == 1:
            y = conformer_conv_mixer(h, cf_in[j], cf_dw[j], cf_dw_b[j], cf_ln_g[j], cf_ln_b[j], cf_out[j])
        elif kind == 2:
            y = fox_attention(h, fox_in[j], fox_bf[j], fox_qn[j], fox_kn[j], fox_out[j])
        else:
            y = moba_attention(h, moba_in[j], moba_qn[j], moba_kn[j], moba_out[j])
        x = x + gt1 * y
        h = rmsnorm(x, ln_ffn_g[i]) * (1.0 + sc2) + sh2
        x = x + gt2 * conv_ffn(h, ffn_up[i], ffn_conv[i], ffn_down[i])
    return x


_drawn_inputs = setup_inputs


def setup_inputs(seed=0):
    import zlib

    import numpy as np

    out = dict(_drawn_inputs(seed))
    spreads = {}
    factors = {'ln_mix_g': 4.511, 'ln_ffn_g': 39.138}
    for name, (base, spread) in spreads.items():
        noise = np.random.default_rng([zlib.crc32(name.encode()), seed]).standard_normal(out[name].shape)
        drawn = base * np.exp(spread * noise) if base else spread * noise
        out[name] = jnp.asarray(drawn.astype(out[name].dtype))
    for name, factor in factors.items():
        out[name] = (out[name] * factor).astype(out[name].dtype)
    return out
```

```python
from contextlib import ExitStack

import concourse.bass as bass
from concourse import mybir

F32 = mybir.dt.float32
F32R = mybir.dt.float32r
BF16 = mybir.dt.bfloat16
ALU = mybir.AluOpType
ACT = mybir.ActivationFunctionType

P = 128
RMS_EPS = 1e-6
HALVES = 2
BLOCK = 512
KIB = 1024


def decoder_layer(nc, x, c, ln_mix_g, ln_ffn_g, ada_w, ada_b, ffn_up, ffn_conv, ffn_down,
                  sc_in, sc_conv, sc_out, out):
    _, SEQ, D = x.shape
    F = ffn_down.shape[1]
    SPAN = SEQ // HALVES
    NK = D // P
    NF = F // P
    NB = SPAN // BLOCK
    NT = SPAN // P
    TB = BLOCK // P
    GROUPS = NF // 2
    TAPS = 3
    assert NB == 2 and NK == 8 and D == 2 * BLOCK and NF % 2 == 0 and GROUPS % 2 == 1

    UB = 3 * NK
    UC = 2 * (NK // 2)
    UP = 4
    UE = 6 * (GROUPS - 1)
    UNITS = UB + UC + UP + UE + 2
    C0, P0, E0, L0 = UB, UB + UC, UB + UC + UP, UB + UC + UP + UE
    assert UNITS % 2 == 0 and UB % 6 == 0

    def slot_of(i):
        return i % 3 if i < C0 else (i - C0 + 3) % 4

    def occupant_of(i):
        j = i - 1
        while slot_of(j % UNITS) != slot_of(i):
            j -= 1
        return j

    x_t = x[0].rearrange("(t p) d -> t p d", p=P)
    out_t = out[0].rearrange("(t p) d -> t p d", p=P)
    sc_in_v = sc_in[0].rearrange("(k p) n -> p k n", p=P)
    up_v = ffn_up[0].rearrange("(k p) n -> p k n", p=P)
    sc_out_v = sc_out[0].rearrange("(k p) n -> p k n", p=P)
    down_v = ffn_down[0].rearrange("(f p) n -> p f n", p=P)
    ada_v = ada_w[0].rearrange("(k p) n -> k p n", p=P)

    with ExitStack() as ctx:
        arena_base = (nc.sbuf_base + 63) // 64 * 64
        arena_bytes = 204 * KIB
        ctx.enter_context(nc.sbuf_tensor("arena", [P, (arena_bytes + 64) // 4], F32))
        at = [arena_base]

        def region(size):
            start = at[0]
            at[0] += (size + 31) // 32 * 32
            assert at[0] <= arena_base + arena_bytes, "arena"
            return start

        def place(name, shape, dt, offset):
            return nc.alloc_sbuf_tensor_at(name, shape, dt, offset=offset)

        h_hi = place("h_hi", [P, NB, NK, BLOCK], F32R, region(32 * KIB))
        h_lo_at = region(32 * KIB)
        h_lo = place("h_lo", [P, NB, NK, BLOCK], F32R, h_lo_at)
        raw = place("raw", [P, 2, D], F32, region(8 * KIB))
        w_hi = place("w_hi", [P, 4, D], F32R, region(16 * KIB))
        w_lo = place("w_lo", [P, 4, D], F32R, region(16 * KIB))
        x1_at = region(32 * KIB)
        x1 = place("x1", [P, NT, D], F32, x1_at)
        Y_at = region(32 * KIB)
        y = place("y", [P, NK, SPAN], F32, Y_at)
        mid_hi = [place(f"mid_hi{p}", [P, 2, SPAN], F32R, Y_at + p * 16 * KIB) for p in range(2)]
        mid_lo = [place(f"mid_lo{p}", [P, 2, SPAN], F32R, Y_at + (16 * p + 8) * KIB) for p in range(2)]
        YS_at = region(16 * KIB)
        y_hi = place("y_hi", [P, 2, 2, BLOCK], F32R, YS_at)
        y_lo = place("y_lo", [P, 2, 2, BLOCK], F32R, YS_at + 8 * KIB)
        us = place("us", [P, 2, SPAN + 8], F32, YS_at)
        gated = place("gated", [P, 2, BLOCK], F32, YS_at + 2 * (SPAN + 8) * 4)
        m_at = x1_at + 32 * KIB - (SPAN + 8) * 4
        m = place("m", [P, SPAN + 8], F32, m_at)
        ada_sum = place("ada_sum", [P, 2, D], F32, x1_at + 16 * KIB)
        stage_y = place("stage_y", [P, TB, D], F32, Y_at + 16 * KIB)
        stage_h = place("stage_h", [P, TB, D], F32, h_lo_at + 16 * KIB)
        ada_tile = [place(f"ada_tile{i}", [P, D], F32,
                          (YS_at if i < 4 else x1_at) + (i % 4) * 4 * KIB) for i in range(8)]
        gate_row = place("gate_row", [P, 2, D], F32, region(8 * KIB))
        scratch_at = region(4 * KIB)
        c_copy = place("c_copy", [P, NB, BLOCK], F32, scratch_at)
        square_out = place("square_out", [P, D], BF16, scratch_at)
        tmp = place("tmp", [P, BLOCK], F32, scratch_at + 2 * KIB)
        ident = place("ident", [P, P], F32, region(512))
        ones = place("ones", [P, P], F32, region(512))
        vec_rows = place("vec_rows", [P, 2, P], F32, region(1024))

        V_ADA, V_C = 0, 6 * NK
        V_GM, V_GF = V_C + NK, V_C + 2 * NK
        V_SC = V_GF + NK
        ROWS0 = V_SC + TAPS * NK
        V_FC, ROWS1 = ROWS0, TAPS * NF
        cols = place("cols", [P, ROWS0 + ROWS1], F32, region(4 * (ROWS0 + ROWS1)))
        cond = place("cond", [P, NK], F32, region(32))
        scale_c = place("scale_c", [P, 2, NK], F32, region(64))
        shift_c = place("shift_c", [P, 2, NK], F32, region(64))
        mod_tmp = place("mod_tmp", [P, NK], F32, region(32))
        sumsq = place("sumsq", [P, 4 * NT], F32, region(128))
        mean_sq = place("mean_sq", [P, 4 * NT], F32, region(128))
        rstd = place("rstd", [P, 4 * NT], F32, region(128))
        minus_half = place("minus_half", [P, 1], F32, region(32))
        m_halo = place("m_halo", [P, NK, 2], F32, region(NK * 8))
        u_halo = place("u_halo", [P, NF, 2], F32, region(NF * 8))

        ps = ctx.enter_context(nc.psum_tensor("ps", [P, 8, BLOCK], F32))

        def sem(name):
            return ctx.enter_context(nc.semaphore(name))

        vec_loaded, gate_bias_loaded = sem("vec_loaded"), sem("gate_bias_loaded")
        const_made, ident_zeroed = sem("const_made"), sem("ident_zeroed")
        vec_transposed, cols_made, cond_made = sem("vec_transposed"), sem("cols_made"), sem("cond_made")
        ada_loaded = [sem(f"ada_loaded{i}") for i in range(8)]
        ada_used, mod_reduced, mod_made = sem("ada_used"), sem("mod_reduced"), sem("mod_made")
        mod_step = sem("mod_step")
        raw_loaded = [sem(f"raw_loaded{i}") for i in range(2)]
        w_hi_made, w_ready, w_used, gate_folded = sem("w_hi_made"), sem("w_ready"), sem("w_used"), sem("gate_folded")
        load_turns, split_turns = sem("load_turns"), sem("split_turns")
        x_staged = [sem(f"x_staged{i}") for i in range(TB)]
        squared, rstd_made, rstd_step = sem("squared"), sem("rstd_made"), sem("rstd_step")
        normed, transposed, modulated = sem("normed"), sem("transposed"), sem("modulated")
        h_hi_made, h_ready = sem("h_hi_made"), sem("h_ready")
        proj_done, c_copied, m_made = sem("proj_done"), sem("c_copied"), sem("m_made")
        m_tapped, conv_step, y_made = sem("m_tapped"), sem("conv_step"), sem("y_made")
        y_hi_made, y_split, y_used = sem("y_hi_made"), sem("y_split"), sem("y_used")
        mixer_done, mixer_scaled, x1_made = sem("mixer_done"), sem("mixer_scaled"), sem("x1_made")
        x1_loaded = [sem(f"x1_loaded{i}") for i in range(NB)]
        up_done, u_tapped, ffn_conv_step = sem("up_done"), sem("u_tapped"), sem("ffn_conv_step")
        convolved, silu_made, gated_made = sem("convolved"), sem("silu_made"), sem("gated_made")
        mid_hi_made, mid_ready = sem("mid_hi_made"), sem("mid_ready")
        down_done, down_added, out_stored = sem("down_done"), sem("down_added"), sem("out_stored")

        VECTORS = [(1, "scale", 0), (0, "shift", 0), (2, "gate", 0),
                   (3, "shift", 1), (4, "scale", 1), (5, "gate", 1)]

        def tile_index(h, stage, t):
            return 2 * NT * h + NT * stage + t

        def stage_of(stage, t):
            return (stage_h if stage == 1 and t < TB else stage_y)[:, t % TB, :]

        def banks_of(stage, t):
            return (4 if stage == 1 and t >= TB else 0) + 2 * (t % 2)

        ITEMS = NF * NB
        DOWNS = 2 * NT
        block = ctx.enter_context(nc.Block())

        @block.sync
        def _(sp):
            def load_raw(r, src, n):
                if not (isinstance(n, int) and n < 2):
                    sp.wait_ge(w_ready, n - 1)
                    sp.sem_inc(load_turns, 1)
                sp.dma_start(raw[:, r, :] if len(src.shape) == 2 else
                             raw[:, r, :].rearrange("p (a b) -> p a b", a=src.shape[1]),
                             src).then_inc(raw_loaded[r], 16)

            def sc_in_stripe(chunk, j):
                return sc_in_v[:, :, bass.ds(((j + 1) % 3) * D + chunk * P, P)]

            def up_stripe(chunk, j):
                return up_v[:, :, bass.ds(j * F + chunk * P, P)]

            def load_x(h, t):
                i = tile_index(h, 0, t)
                if t >= TB:
                    sp.wait_ge(h_ready, i - TB + 1)
                elif h > 0:
                    sp.wait_ge(down_done, DOWNS * (GROUPS * h - 1))
                sp.dma_start(stage_y[:, t % TB, :], x_t[NT * h + t]).then_inc(x_staged[t % TB], 16)

            def load_b(U, pair):
                for j in range(6):
                    load_raw(j % 2, sc_in_stripe(2 * pair + j // 3, j % 3), U + 6 * pair + j)

            for h in range(HALVES):
                U = UNITS * h
                if h == 0:
                    for t in range(TB):
                        load_x(h, t)
                    load_raw(0, sc_in_stripe(0, 0), 0)
                    load_raw(1, sc_in_stripe(0, 1), 1)
                for t in range(TB, NT):
                    load_x(h, t)
                for j in range(2, 6):
                    load_raw(j % 2, sc_in_stripe(j // 3, j % 3), U + j)
                with sp.Fori(1, NK // 2) as pair:
                    load_b(U, pair)
                for i in range(UC):
                    dh, s = divmod(i, NK // 2)
                    load_raw(i % 2, sc_out_v[:, 2 * s:2 * s + 2, dh * BLOCK:(dh + 1) * BLOCK], U + C0 + i)
                    if i == 4:
                        sp.wait_ge(y_made, NK * NB * (h + 1))
                        for b in range(NB):
                            sp.dma_start(x1[:, TB * b:TB * b + TB, :],
                                         x_t[NT * h + TB * b:NT * h + TB * b + TB].rearrange("t p d -> p t d")
                                         ).then_inc(x1_loaded[b], 16)
                for i in range(UP):
                    load_raw(i % 2, up_stripe(i // 2, i % 2), U + P0 + i)
                with sp.Fori(0, (GROUPS - 1) // 2) as g2:
                    for e in range(2):
                        for i in range(4):
                            load_raw(i % 2, up_stripe(4 * g2 + 2 * e + 2 + i // 2, i % 2),
                                     U + E0 + 12 * g2 + 6 * e + i)
                        for i in range(2):
                            load_raw(i % 2, down_v[:, bass.ds(4 * g2 + 2 * e + i, 1), :],
                                     U + E0 + 12 * g2 + 6 * e + 4 + i)
                for i in range(2):
                    load_raw(i % 2, down_v[:, 2 * (GROUPS - 1) + i, :], U + L0 + i)
                if h + 1 < HALVES:
                    for t in range(TB):
                        load_x(h + 1, t)
                    load_raw(0, sc_in_stripe(0, 0), U + UNITS)
                    load_raw(1, sc_in_stripe(0, 1), U + UNITS + 1)
                for t in range(NT):
                    sp.wait_ge(down_added, DOWNS * (GROUPS * (h + 1) - 1) + 2 * t + 2 + 4)
                    sp.dma_start(out_t[NT * h + t], x1[:, t, :]).then_inc(out_stored, 16)
            sp.wait_ge(out_stored, 16 * NT * HALVES)

        @block.gpsimd
        def _(pool):
            pool.memset(ident[:], 0.0).then_inc(ident_zeroed, 1)
            pool.memset(ones[:], 1.0)
            pool.memset(minus_half[:], -0.5)
            pool.memset(m_halo[:], 0.0)
            pool.memset(u_halo[:], 0.0)
            pool.wait_ge(ident_zeroed, 1)
            pool.affine_select(out=ident[:], in_=ident[:], compare_op=ALU.not_equal, fill=1.0,
                               base=0, pattern=[[-1, P]], channel_multiplier=1).then_inc(const_made, 1)
            def split(n, n2, slot, used, gate=None):
                r, m = n2
                pool.wait_ge(raw_loaded[r], 16 * (m + 1))
                if used is not None:
                    pool.wait_ge(w_used, used)
                if gate is not None:
                    pool.tensor_tensor(raw[:, r, :], raw[:, r, :], gate_row[:, 1, :], ALU.mult).then_inc(gate_folded, 1)
                    pool.wait_ge(gate_folded, gate)
                pool.sem_inc(split_turns, 1)
                pool.tensor_copy(w_hi[:, slot, :], raw[:, r, :]).then_inc(w_hi_made, 1)
                pool.wait_ge(w_hi_made, n + 1)
                pool.tensor_tensor(w_lo[:, slot, :], raw[:, r, :], w_hi[:, slot, :].bitcast(F32),
                                   ALU.subtract).then_inc(w_ready, 1)

            def take_rstd(h, stage, t):
                i = tile_index(h, stage, t)
                pool.wait_ge(squared, i + 1)
                pool.tensor_scalar(mean_sq[:, i:i + 1], sumsq[:, i:i + 1], 1.0 / D, RMS_EPS,
                                   ALU.mult, ALU.add).then_inc(rstd_step, 1)
                pool.wait_ge(rstd_step, i + 1)
                pool.tensor_tensor(rstd[:, i:i + 1], mean_sq[:, i:i + 1], minus_half[:], ALU.pow).then_inc(rstd_made, 1)

            def make_h_lo(h, stage, t):
                i = tile_index(h, stage, t)
                b, tt = divmod(t, TB)
                cut = slice(tt * P, tt * P + P)
                pool.wait_ge(h_hi_made, i + 1)
                pool.tensor_tensor(h_lo[:, b, :, cut], stage_of(stage, t).rearrange("p (k n) -> p k n", k=NK),
                                   h_hi[:, b, :, cut].bitcast(F32), ALU.subtract).then_inc(h_ready, 1)

            def split_at(U, i, extra=0, extra_raw=0, gate=None):
                o = occupant_of(i)
                used = None if U + o < 0 else U + o + 1 + extra
                split(U + i + extra, (i % 2, (U + i) // 2 + extra_raw), slot_of(i), used, gate)

            for h in range(HALVES):
                U = UNITS * h
                for t in range(TB):
                    take_rstd(h, 0, t)
                for i in range(2):
                    split_at(U, i)
                make_h_lo(h, 0, 0)
                for t in range(1, TB + 1):
                    make_h_lo(h, 0, t)
                    take_rstd(h, 0, t + TB - 1)
                for t in range(TB + 1, NT):
                    make_h_lo(h, 0, t)
                for i in range(2, 6):
                    split_at(U, i)
                with pool.Fori(0, NK // 2 - 1) as pair:
                    for i in range(6, 12):
                        split_at(U, i, 6 * pair, 3 * pair)
                for i in range(C0, P0):
                    split_at(U, i)
                take_rstd(h, 1, 0)
                take_rstd(h, 1, 1)
                split_at(U, P0)
                take_rstd(h, 1, 2)
                take_rstd(h, 1, 3)
                make_h_lo(h, 1, 0)
                make_h_lo(h, 1, 1)
                split_at(U, P0 + 1)
                make_h_lo(h, 1, 2)
                make_h_lo(h, 1, 3)
                split_at(U, P0 + 2)
                take_rstd(h, 1, TB)
                take_rstd(h, 1, TB + 1)
                split_at(U, P0 + 3)
                take_rstd(h, 1, TB + 2)
                take_rstd(h, 1, TB + 3)
                for t in range(TB, NT):
                    make_h_lo(h, 1, t)
                if h == 0:
                    pool.wait_ge(mod_made, len(VECTORS))
                folded = 2 * GROUPS * h
                with pool.Fori(0, (GROUPS - 1) // 2) as g2:
                    for j in range(12):
                        e, i = divmod(j, 6)
                        split_at(U, E0 + j, 12 * g2, 6 * g2,
                                 gate=folded + 4 * g2 + 2 * e + i - 4 + 1 if i >= 4 else None)
                for i in range(2):
                    split_at(U, L0 + i, gate=folded + 2 * (GROUPS - 1) + i + 1)

        @block.scalar
        def _(act):
            def load_ada(n):
                v = VECTORS[n][0]
                for k in range(NK):
                    if n > 0:
                        act.wait_ge(ada_used, NK * (n - 1) + k + 1)
                    act.dma_start(ada_tile[k][:], ada_v[k][:, v * D:(v + 1) * D]).then_inc(ada_loaded[k], 16)

            def rows(dst, src):
                act.dma_start(dst, src.rearrange("(r n) -> r n", n=P)).then_inc(vec_loaded, 16)

            def square(h, stage, t):
                i = tile_index(h, stage, t)
                if stage == 0:
                    act.wait_ge(x_staged[t % TB], 16 * (2 * h + t // TB + 1))
                    src = stage_y[:, t % TB, :]
                else:
                    act.wait_ge(x1_made, 2 * NT * h + NT + t + 1)
                    src = x1[:, t, :]
                if i > 0:
                    act.wait_ge(squared, i)
                act.activation(square_out[:], src, ACT.Square, accum_out=sumsq[:, i:i + 1]).then_inc(squared, 1)

            def norm(h, stage, t):
                i = tile_index(h, stage, t)
                act.wait_ge(rstd_made, i + 1)
                src = stage_y[:, t % TB, :] if stage == 0 else x1[:, t, :]
                act.activation(stage_of(stage, t), src, ACT.Copy, scale=rstd[:, i:i + 1]).then_inc(normed, 1)

            def make_h_hi(h, stage, t):
                i = tile_index(h, stage, t)
                b, tt = divmod(t, TB)
                act.wait_ge(modulated, i + 1)
                act.activation(h_hi[:, b, :, tt * P:tt * P + P],
                               stage_of(stage, t).rearrange("p (k n) -> p k n", k=NK), ACT.Copy).then_inc(h_hi_made, 1)

            def stage_b(h, chunk):
                N = NB * NK * h
                for b in range(NB):
                    act.wait_ge(proj_done, 6 * NK * h + 6 * chunk + b + 1)
                    act.activation(c_copy[:, b, :], ps[:, 4 + b, :], ACT.Copy).then_inc(c_copied, 1)
                for b in range(NB):
                    act.wait_ge(m_made, N + NB * chunk + b + 1)
                    act.activation(y[:, bass.ds(chunk, 1), b * BLOCK:(b + 1) * BLOCK],
                                   m[:, 2 + b * BLOCK:2 + (b + 1) * BLOCK].unsqueeze(1), ACT.Copy,
                                   scale=cols[:, bass.ds(V_SC + 2 * NK + chunk, 1)]).then_inc(m_tapped, 1)

            def make_y_hi(h, n):
                dh, grp, s = n // 8, n // 4 % 2, n % 4
                if n >= 2:
                    act.wait_ge(y_used, 15 * h + n - 1)
                act.activation(y_hi[:, n % 2], y[:, 2 * s:2 * s + 2, grp * BLOCK:(grp + 1) * BLOCK],
                               ACT.Copy).then_inc(y_hi_made, 1)

            def ffn_item(h, q, qe, chunk, chunk_e, b, par, j):
                Q = ITEMS * h + q + qe
                pp = q % 2
                u_bank, ce = 2 * pp, chunk + chunk_e
                act.wait_ge(up_done, 2 * Q + 1)
                if b == 0:
                    act.activation(us[:, j, 0:2], u_halo[:, bass.ds(ce, 1), :].rearrange("p a b -> p (a b)"), ACT.Copy)
                act.activation(us[:, j, 2 + b * BLOCK:2 + (b + 1) * BLOCK], ps[:, u_bank, :], ACT.Copy)
                if b == NB - 1 and h + 1 < HALVES:
                    act.activation(u_halo[:, bass.ds(ce, 1), :].rearrange("p a b -> p (a b)"),
                                   ps[:, u_bank, BLOCK - 2:BLOCK], ACT.Copy)
                act.activation(gated[:, pp, :], ps[:, u_bank, :], ACT.Copy,
                               scale=cols[:, bass.ds(V_FC + 2 * NF + ce, 1)]).then_inc(u_tapped, 1)
                act.wait_ge(convolved, Q + 1)
                act.activation(gated[:, pp, :], gated[:, pp, :], ACT.Silu).then_inc(silu_made, 1)
                act.wait_ge(gated_made, Q + 1)
                act.activation(mid_hi[par][:, j, b * BLOCK:(b + 1) * BLOCK], gated[:, pp, :], ACT.Copy).then_inc(mid_hi_made, 1)

            act.wait_ge(const_made, 1)
            rows(vec_rows[V_ADA:V_C, 0, :], ada_b[0])
            rows(vec_rows[V_C:V_GM, 0, :], c[0])
            rows(vec_rows[V_GM:V_GF, 0, :], ln_mix_g[0])
            rows(vec_rows[V_GF:V_SC, 0, :], ln_ffn_g[0])
            rows(vec_rows[V_SC:ROWS0, 0, :], sc_conv[0].rearrange("a n -> (a n)"))
            rows(vec_rows[0:ROWS1, 1, :], ffn_conv[0].rearrange("a n -> (a n)"))
            load_ada(0)
            for i, v in enumerate((2, 5)):
                act.dma_start(gate_row[:, i, :], ada_b[:, v * D:(v + 1) * D].broadcast_to([P, D])).then_inc(gate_bias_loaded, 16)
            act.wait_ge(cols_made, 1)
            act.activation(cond[:], cols[:, V_C:V_GM], ACT.Silu).then_inc(cond_made, 1)
            for t in range(2):
                square(0, 0, t)
            load_ada(1)
            for h in range(HALVES):
                if h > 0:
                    square(h, 0, 0)
                    square(h, 0, 1)
                norm(h, 0, 0)
                for t in range(2, TB):
                    square(h, 0, t)
                    norm(h, 0, t - 1)
                norm(h, 0, TB - 1)
                make_h_hi(h, 0, 0)
                for t in range(1, TB + 1):
                    make_h_hi(h, 0, t)
                    square(h, 0, t + TB - 1)
                    norm(h, 0, t + TB - 1)
                for t in range(TB + 1, NT):
                    make_h_hi(h, 0, t)
                if h == 0:
                    for chunk in range(4):
                        load_ada(2 + chunk)
                        stage_b(h, chunk)
                    with act.Fori(4, NK) as chunk:
                        stage_b(h, chunk)
                else:
                    with act.Fori(0, NK) as chunk:
                        stage_b(h, chunk)
                act.wait_ge(y_made, NB * NK * (h + 1))
                for n in range(14):
                    make_y_hi(h, n)
                square(h, 1, 0)
                square(h, 1, 1)
                norm(h, 1, 0)
                make_y_hi(h, 14)
                norm(h, 1, 1)
                square(h, 1, 2)
                square(h, 1, 3)
                norm(h, 1, 2)
                make_y_hi(h, 15)
                norm(h, 1, 3)
                for t in range(TB):
                    make_h_hi(h, 1, t)
                square(h, 1, TB)
                square(h, 1, TB + 1)
                norm(h, 1, TB)
                square(h, 1, TB + 2)
                norm(h, 1, TB + 1)
                square(h, 1, TB + 3)
                norm(h, 1, TB + 2)
                norm(h, 1, TB + 3)
                make_h_hi(h, 1, TB)
                ffn_item(h, 0, 0, 0, 0, 0, 0, 0)
                for t in range(TB + 1, NT):
                    make_h_hi(h, 1, t)
                ffn_item(h, 1, 0, 1, 0, 0, 0, 1)
                ffn_item(h, 2, 0, 0, 0, 1, 0, 0)
                ffn_item(h, 3, 0, 1, 0, 1, 0, 1)
                with act.Fori(0, (GROUPS - 1) // 2) as g2:
                    for e in range(2):
                        for i in range(4):
                            ffn_item(h, 4 + 4 * e + i, 8 * g2, 2 + 2 * e + i // 2, 4 * g2, i % 2, 1 - e, i // 2)

        @block.vector
        def _(dve):
            def ada_vector(n):
                s = ada_sum[:, n % 2, :]
                if n >= 2:
                    dve.wait_ge(mod_reduced, n - 1)
                for k in range(NK):
                    dve.wait_ge(ada_loaded[k], 16 * (n + 1))
                    if k == 0:
                        dve.tensor_scalar(s, ada_tile[k][:], cond[:, k:k + 1], None, ALU.mult).then_inc(ada_used, 1)
                    else:
                        dve.wait_ge(ada_used, NK * n + k)
                        dve.scalar_tensor_tensor(out=s, in0=ada_tile[k][:], scalar=cond[:, k:k + 1], in1=s,
                                                 op0=ALU.mult, op1=ALU.add).then_inc(ada_used, 1)

            def mod_vector(n):
                v, kind, which = VECTORS[n]
                bias = cols[:, V_ADA + v * NK:V_ADA + (v + 1) * NK]
                dve.wait_ge(mod_reduced, n + 1)
                if kind == "gate":
                    dve.wait_ge(gate_bias_loaded, 32)
                    dve.tensor_tensor(gate_row[:, which, 0:BLOCK], ps[:, 2, :], gate_row[:, which, 0:BLOCK], ALU.add)
                    dve.tensor_tensor(gate_row[:, which, BLOCK:D], ps[:, 3, :], gate_row[:, which, BLOCK:D],
                                      ALU.add).then_inc(mod_made, 1)
                elif kind == "shift":
                    dve.tensor_tensor(shift_c[:, which, :], ps[:, 2, 0:NK], bias, ALU.add).then_inc(mod_made, 1)
                else:
                    gain = cols[:, V_GF:V_SC] if which else cols[:, V_GM:V_GF]
                    dve.tensor_tensor(mod_tmp[:], ps[:, 2, 0:NK], bias, ALU.add).then_inc(mod_step, 1)
                    dve.wait_ge(mod_step, which + 1)
                    dve.scalar_tensor_tensor(out=scale_c[:, which, :], in0=mod_tmp[:], scalar=1.0, in1=gain,
                                             op0=ALU.add, op1=ALU.mult).then_inc(mod_made, 1)

            def modulate(h, stage, t):
                i = tile_index(h, stage, t)
                bank = banks_of(stage, t)
                dst = stage_of(stage, t)
                dve.wait_ge(transposed, i + 1)
                for k in range(NK):
                    op = dve.tensor_scalar(dst[:, k * P:(k + 1) * P],
                                           ps[:, bank + k // 4, (k % 4) * P:(k % 4 + 1) * P],
                                           scale_c[:, stage, k:k + 1], shift_c[:, stage, k:k + 1], ALU.mult, ALU.add)
                op.then_inc(modulated, 1)

            def stage_b(h, chunk):
                N = NB * NK * h

                def tap(w):
                    return cols[:, bass.ds(V_SC + w * NK + chunk, 1)]

                def yb(b):
                    return y[:, bass.ds(chunk, 1), b * BLOCK:(b + 1) * BLOCK].rearrange("p a n -> p (a n)")

                halo = m_halo[:, bass.ds(chunk, 1), :].rearrange("p a n -> p (a n)")
                dve.tensor_copy(m[:, 0:2], halo)
                for b in range(NB):
                    dve.wait_ge(c_copied, N + NB * chunk + b + 1)
                    dve.wait_ge(proj_done, 6 * NK * h + 6 * chunk + NB + b + 1)
                    dve.tensor_tensor(m[:, 2 + b * BLOCK:2 + (b + 1) * BLOCK], ps[:, 6 + b, :], c_copy[:, b, :],
                                      ALU.mult).then_inc(m_made, 1)
                for b in range(NB):
                    dve.wait_ge(m_tapped, N + NB * chunk + b + 1)
                    dve.scalar_tensor_tensor(out=yb(b), in0=m[:, 1 + b * BLOCK:1 + (b + 1) * BLOCK], scalar=tap(1),
                                             in1=yb(b), op0=ALU.mult, op1=ALU.add).then_inc(conv_step, 1)
                if h + 1 < HALVES:
                    dve.tensor_copy(halo, m[:, SPAN:SPAN + 2])
                for b in range(NB):
                    dve.wait_ge(conv_step, 2 * N + 2 * NB * chunk + b + 1)
                    dve.scalar_tensor_tensor(out=yb(b), in0=m[:, b * BLOCK:(b + 1) * BLOCK], scalar=tap(0),
                                             in1=yb(b), op0=ALU.mult, op1=ALU.add).then_inc(conv_step, 1)
                for b in range(NB):
                    dve.wait_ge(conv_step, 2 * N + 2 * NB * chunk + NB + b + 1)
                    dve.wait_ge(proj_done, 6 * NK * h + 6 * chunk + 2 * NB + b + 1)
                    dve.tensor_tensor(yb(b), ps[:, b, :], yb(b), ALU.mult).then_inc(y_made, 1)

            def make_y_lo(h, n):
                grp, s = n // 4 % 2, n % 4
                dve.wait_ge(y_hi_made, 16 * h + n + 1)
                dve.tensor_tensor(y_lo[:, n % 2], y[:, 2 * s:2 * s + 2, grp * BLOCK:(grp + 1) * BLOCK],
                                  y_hi[:, n % 2].bitcast(F32), ALU.subtract).then_inc(y_split, 1)

            def residual(h, group):
                dh, grp = divmod(group, 2)
                cut = slice(dh * BLOCK, (dh + 1) * BLOCK)
                if h == 0 and group == 0:
                    dve.wait_ge(mod_made, len(VECTORS))
                if dh == 0:
                    dve.wait_ge(x1_loaded[grp], 16 * (h + 1))
                for i in range(TB):
                    n = 16 * h + 4 * group + i
                    t = TB * grp + i
                    dve.wait_ge(mixer_done, n + 1)
                    if n > 0:
                        dve.wait_ge(x1_made, n)
                    dve.tensor_tensor(tmp[:], ps[:, 4 + i, :], gate_row[:, 0, cut], ALU.mult).then_inc(mixer_scaled, 1)
                    dve.wait_ge(mixer_scaled, n + 1)
                    dve.tensor_tensor(x1[:, t, cut], tmp[:], x1[:, t, cut], ALU.add).then_inc(x1_made, 1)

            def ffn_item(h, q, qe, chunk, chunk_e, b, par, j):
                Q = ITEMS * h + q + qe
                pp = q % 2
                ce = chunk + chunk_e
                g = gated[:, pp, :]

                def tap(w):
                    return cols[:, bass.ds(V_FC + w * NF + ce, 1)]

                dve.wait_ge(u_tapped, Q + 1)
                dve.scalar_tensor_tensor(out=g, in0=us[:, j, 1 + b * BLOCK:1 + (b + 1) * BLOCK], scalar=tap(1),
                                         in1=g, op0=ALU.mult, op1=ALU.add).then_inc(ffn_conv_step, 1)
                dve.wait_ge(ffn_conv_step, Q + 1)
                dve.scalar_tensor_tensor(out=g, in0=us[:, j, b * BLOCK:(b + 1) * BLOCK], scalar=tap(0),
                                         in1=g, op0=ALU.mult, op1=ALU.add).then_inc(convolved, 1)
                dve.wait_ge(silu_made, Q + 1)
                dve.wait_ge(up_done, 2 * Q + 2)
                dve.tensor_tensor(g, ps[:, 2 * pp + 1, :], g, ALU.mult).then_inc(gated_made, 1)
                dve.wait_ge(mid_hi_made, Q + 1)
                cut = slice(b * BLOCK, (b + 1) * BLOCK)
                dve.tensor_tensor(mid_lo[par][:, j, cut], g, mid_hi[par][:, j, cut].bitcast(F32),
                                  ALU.subtract).then_inc(mid_ready, 1)

            def add_down(h, g, ge):
                N = DOWNS * (GROUPS * h + g + ge)
                for r in range(DOWNS):
                    t, dh = divmod(r, 2)
                    cut = slice(dh * BLOCK, (dh + 1) * BLOCK)
                    dve.wait_ge(down_done, N + r + 1)
                    dve.tensor_tensor(x1[:, t, cut], ps[:, 4 + r % 4, :], x1[:, t, cut], ALU.add).then_inc(down_added, 1)

            dve.sem_inc(down_added, 4)
            dve.wait_ge(const_made, 1)
            dve.wait_ge(vec_transposed, 1)
            dve.tensor_copy(cols[:], ps[:, 2, 0:ROWS0 + ROWS1]).then_inc(cols_made, 1)
            dve.wait_ge(cond_made, 1)
            ada_vector(0)
            mod_vector(0)
            ada_vector(1)
            mod_vector(1)
            dve.wait_ge(mod_made, 2)
            for h in range(HALVES):
                for t in range(NT):
                    modulate(h, 0, t)
                if h == 0:
                    for chunk in range(4):
                        ada_vector(2 + chunk)
                        stage_b(h, chunk)
                        mod_vector(2 + chunk)
                    with dve.Fori(4, NK) as chunk:
                        stage_b(h, chunk)
                else:
                    dve.wait_ge(out_stored, 16 * NT * h)
                    with dve.Fori(0, NK) as chunk:
                        stage_b(h, chunk)
                for n in range(16):
                    make_y_lo(h, n)
                    if n % 4 == 0 and n > 0:
                        residual(h, n // 4 - 1)
                for t in range(TB):
                    modulate(h, 1, t)
                residual(h, 3)
                modulate(h, 1, TB)
                ffn_item(h, 0, 0, 0, 0, 0, 0, 0)
                for t in range(TB + 1, NT):
                    modulate(h, 1, t)
                ffn_item(h, 1, 0, 1, 0, 0, 0, 1)
                ffn_item(h, 2, 0, 0, 0, 1, 0, 0)
                ffn_item(h, 3, 0, 1, 0, 1, 0, 1)
                with dve.Fori(0, (GROUPS - 1) // 2) as g2:
                    for e in range(2):
                        for i in range(4):
                            ffn_item(h, 4 + 4 * e + i, 8 * g2, 2 + 2 * e + i // 2, 4 * g2, i % 2, 1 - e, i // 2)
                        add_down(h, e, 2 * g2)
                add_down(h, GROUPS - 1, 0)

        @block.tensor
        def _(pe):
            def products(bank, pairs, start=True, stop=True, gone=(), first_done=None):
                last = len(pairs) - 1
                gone = list(gone)
                for i, ((s_hi, s_lo), (v_hi, v_lo)) in enumerate(pairs):
                    a = pe.matmul(ps[:, bank, :], s_hi, v_hi, start=start and i == 0, stop=False)
                    b = pe.matmul(ps[:, bank, :], s_hi, v_lo, start=False, stop=False)
                    op = pe.matmul(ps[:, bank, :], s_lo, v_hi, start=False, stop=stop and i == last)
                    if i == 0:
                        for done, signal in zip((a, b), gone):
                            done.then_inc(signal, 1)
                        if first_done is not None:
                            op.then_inc(first_done, 1)
                return op

            def project(slot, b, bank, gone=()):
                return products(bank, [((w_hi[:, slot, k * P:(k + 1) * P], w_lo[:, slot, k * P:(k + 1) * P]),
                                        (h_hi[:, b, k, :], h_lo[:, b, k, :])) for k in range(NK)], gone=gone)

            def transpose_tile(h, stage, t, gone=None):
                i = tile_index(h, stage, t)
                bank = banks_of(stage, t)
                src = stage_of(stage, t)
                pe.wait_ge(normed, i + 1)
                if h == 0 and stage == 0 and t == 1:
                    pe.wait_ge(mod_made, 2)
                if stage == 1 and t == TB:
                    pe.wait_ge(x1_made, 16 * h + 16)
                if t % TB >= 2 or (stage == 0 and t >= 2):
                    pe.wait_ge(modulated, i - 1)
                for k in range(NK):
                    op = pe.transpose(ps[:, bank + k // 4, (k % 4) * P:(k % 4 + 1) * P],
                                      src[:, k * P:(k + 1) * P], ident[:])
                    if k == 0 and gone is not None:
                        op.then_inc(gone, 1)
                op.then_inc(transposed, 1)

            def reduce_mod(n):
                pe.wait_ge(ada_used, NK * (n + 1))
                if n > 0:
                    pe.wait_ge(mod_made, n)
                if VECTORS[n][1] == "gate":
                    for i in range(2):
                        op = pe.matmul(ps[:, 2 + i, :], ones[:], ada_sum[:, n % 2, i * BLOCK:(i + 1) * BLOCK],
                                       start=True, stop=True)
                else:
                    for k in range(NK):
                        op = pe.matmul(ps[:, 2, k:k + 1], ada_sum[:, n % 2, k * P:(k + 1) * P], ones[:, 0:1],
                                       start=True, stop=True)
                op.then_inc(mod_reduced, 1)

            def stage_b(h, chunk, first=False):
                N = NB * NK * h
                free = (c_copied, m_made, y_made)
                for j in range(3):
                    pe.wait_ge(w_ready, UNITS * h + 3 * chunk + j + 1)
                    for b in range(NB):
                        if first and j == 0:
                            pe.wait_ge(h_ready, tile_index(h, 0, TB * b + TB - 1) + 1)
                            if h > 0 and b == 0:
                                pe.wait_ge(down_added, DOWNS * GROUPS * h + 4)
                        if not first:
                            pe.wait_ge(free[j], N + NB * (chunk - 1) + b + 1)
                        gone = (w_used,) if b == 0 and not (first and j == 0) else ()
                        project(j, b, (4, 6, 0)[j] + b, gone).then_inc(proj_done, 1)

            def mixer_step(h, n):
                dh, grp, s = n // 8, n // 4 % 2, n % 4
                slot = slot_of(C0 + 4 * dh + s)
                gone = [y_used] if n > 0 else [w_used]
                if n > 0 and (n - 1) // 4 % 2 == 1:
                    gone.append(w_used)
                if grp == 0:
                    pe.wait_ge(w_ready, UNITS * h + C0 + 4 * dh + s + 1)
                pe.wait_ge(y_split, 16 * h + n + 1)
                for i in range(TB):
                    if s == 0 and n > 0:
                        pe.wait_ge(x1_made, 16 * h + n - TB + i + 1)
                    cut = slice(i * P, (i + 1) * P)
                    op = products(4 + i, [((y_hi[:, n % 2, kk, cut], y_lo[:, n % 2, kk, cut]),
                                           (w_hi[:, slot, kk * BLOCK:(kk + 1) * BLOCK],
                                            w_lo[:, slot, kk * BLOCK:(kk + 1) * BLOCK])) for kk in range(2)],
                                  s == 0, s == 3, gone if i == 0 else ())
                    if s == 3:
                        op.then_inc(mixer_done, 1)

            def up_part(h, q, qe, i, ie, j, b, gone):
                if j == 0 and q >= 2:
                    pe.wait_ge(gated_made, ITEMS * h + q + qe - 1)
                if b == 0:
                    pe.wait_ge(w_ready, UNITS * h + i + ie + 1)
                project(slot_of(i), b, 2 * (q % 2) + j, (w_used,) if gone else ()).then_inc(up_done, 1)

            def down(h, g, ge, i, ie, par):
                N = DOWNS * (GROUPS * h + g + ge)
                slots = slot_of(i), slot_of(i + 1)
                pe.wait_ge(w_ready, UNITS * h + i + ie + 2)
                pe.wait_ge(mid_ready, ITEMS * h + 4 * (g + ge) + 4)
                for r in range(DOWNS):
                    t, dh = divmod(r, 2)
                    cut = slice(t * P, (t + 1) * P)
                    pe.wait_ge(down_added, N + r + 1)
                    products(4 + r % 4, [((mid_hi[par][:, j, cut], mid_lo[par][:, j, cut]),
                                          (w_hi[:, slots[j], dh * BLOCK:(dh + 1) * BLOCK],
                                           w_lo[:, slots[j], dh * BLOCK:(dh + 1) * BLOCK])) for j in range(2)],
                             gone=(w_used,) if r == 0 else (),
                             first_done=w_used if r == DOWNS - 1 else None).then_inc(down_done, 1)

            pe.wait_ge(const_made, 1)
            pe.wait_ge(vec_loaded, 16 * 6)
            pe.transpose(ps[:, 2, 0:ROWS0], vec_rows[0:ROWS0, 0, :], ident[0:ROWS0, 0:ROWS0])
            pe.transpose(ps[:, 2, ROWS0:ROWS0 + ROWS1], vec_rows[0:ROWS1, 1, :], ident[0:ROWS1, 0:ROWS1]
                         ).then_inc(vec_transposed, 1)
            pe.wait_ge(cols_made, 1)
            reduce_mod(0)
            reduce_mod(1)
            for h in range(HALVES):
                for t in range(NT):
                    transpose_tile(h, 0, t, w_used if h > 0 and t == 0 else None)
                if h == 0:
                    for chunk in range(4):
                        stage_b(h, chunk, chunk == 0)
                        reduce_mod(2 + chunk)
                    with pe.Fori(4, NK) as chunk:
                        stage_b(h, chunk)
                else:
                    stage_b(h, 0, True)
                    with pe.Fori(1, NK) as chunk:
                        stage_b(h, chunk)
                for n in range(14):
                    mixer_step(h, n)
                transpose_tile(h, 1, 0)
                transpose_tile(h, 1, 1)
                mixer_step(h, 14)
                transpose_tile(h, 1, 2)
                transpose_tile(h, 1, 3)
                mixer_step(h, 15)
                pe.wait_ge(h_ready, tile_index(h, 1, TB - 1) + 1)
                up_part(h, 0, 0, P0, 0, 0, 0, True)
                up_part(h, 0, 0, P0 + 1, 0, 1, 0, False)
                transpose_tile(h, 1, TB)
                up_part(h, 1, 0, P0 + 2, 0, 0, 0, False)
                transpose_tile(h, 1, TB + 1)
                transpose_tile(h, 1, TB + 2)
                up_part(h, 1, 0, P0 + 3, 0, 1, 0, False)
                transpose_tile(h, 1, TB + 3)
                pe.wait_ge(h_ready, tile_index(h, 1, NT - 1) + 1)
                for i in range(4):
                    up_part(h, 2 + i // 2, 0, P0 + i, 0, i % 2, 1, i > 0)
                with pe.Fori(0, (GROUPS - 1) // 2) as g2:
                    for e in range(2):
                        for i in range(4):
                            b = i % 2
                            unit = E0 + 6 * e + 2 * (i // 2)
                            up_part(h, 4 + 4 * e + i, 8 * g2, unit, 12 * g2, 0, b, b == 0)
                            up_part(h, 4 + 4 * e + i, 8 * g2, unit + 1, 12 * g2, 1, b, b == 1)
                        down(h, e, 2 * g2, E0 + 6 * e + 4, 12 * g2, e)
                down(h, GROUPS - 1, 0, L0, 0, 0)


_INS = ['x', 'c', 'ln_mix_g', 'ln_ffn_g', 'ada_w', 'ada_b', 'ffn_up', 'ffn_conv', 'ffn_down', 'sc_in', 'sc_conv', 'sc_out']


def kernel(**inputs):
    import numpy as _np
    import concourse.bacc as _bacc
    from concourse import mybir as _mybir
    from concourse.bass_utils import run_bass_kernel_spmd as _run

    nc = _bacc.Bacc("TRN2", target_bir_lowering=False, num_devices=1)
    arrays, args = {}, []
    for name in _INS:
        a = _np.ascontiguousarray(inputs[name])
        arrays[f"in_{name}_dram"] = a
        args.append(nc.dram_tensor(f"in_{name}_dram", a.shape, _mybir.dt.from_np(a.dtype), kind="ExternalInput").ap())
    shape = inputs["x"].shape
    args.append(nc.dram_tensor("out_0_dram", shape, _mybir.dt.float32, kind="ExternalOutput").ap())
    decoder_layer(nc, *args)
    r = _run(nc, [arrays], core_ids=[0])
    return r.results[0]["out_0_dram"]
```

```python
from contextlib import ExitStack

import concourse.bass as bass
from concourse import mybir

F32 = mybir.dt.float32
F32R = mybir.dt.float32r
BF16 = mybir.dt.bfloat16
ALU = mybir.AluOpType
ACT = mybir.ActivationFunctionType

P = 128
RMS_EPS = 1e-6
HALVES = 2
BLOCK = 512
KIB = 1024


def decoder_layer(nc, x, c, ln_mix_g, ln_ffn_g, ada_w, ada_b, ffn_up, ffn_conv, ffn_down,
                  sc_in, sc_conv, sc_out, out):
    _, SEQ, D = x.shape
    F = ffn_down.shape[1]
    SPAN = SEQ // HALVES
    NK = D // P
    NF = F // P
    NB = SPAN // BLOCK
    NT = SPAN // P
    TB = BLOCK // P
    GROUPS = NF // 2
    TAPS = 3
    assert NB == 2 and NK == 8 and D == 2 * BLOCK and NF % 2 == 0 and GROUPS % 2 == 1

    UB = 3 * NK
    UC = 2 * (NK // 2)
    UP = 4
    UE = 6 * (GROUPS - 1)
    UNITS = UB + UC + UP + UE + 2
    C0, P0, E0, L0 = UB, UB + UC, UB + UC + UP, UB + UC + UP + UE
    assert UNITS % 2 == 0 and UB % 6 == 0

    def slot_of(i):
        if i < C0:
            return i % 3
        return (3, 0, 1, 2)[i % 4] if i < P0 else (3, 2, 0, 1)[(i - P0) % 4]

    def occupant_of(i):
        j = i - 1
        while slot_of(j % UNITS) != slot_of(i):
            j -= 1
        return j

    x_t = x[0].rearrange("(t p) d -> t p d", p=P)
    out_t = out[0].rearrange("(t p) d -> t p d", p=P)
    sc_in_v = sc_in[0].rearrange("(k p) n -> p k n", p=P)
    up_v = ffn_up[0].rearrange("(k p) n -> p k n", p=P)
    sc_out_v = sc_out[0].rearrange("(k p) n -> p k n", p=P)
    down_v = ffn_down[0].rearrange("(f p) n -> p f n", p=P)
    ada_v = ada_w[0].rearrange("(k p) n -> k p n", p=P)

    with ExitStack() as ctx:
        arena_base = (nc.sbuf_base + 63) // 64 * 64
        arena_bytes = 204 * KIB
        ctx.enter_context(nc.sbuf_tensor("arena", [P, (arena_bytes + 64) // 4], F32))
        at = [arena_base]

        def region(size):
            start = at[0]
            at[0] += (size + 31) // 32 * 32
            assert at[0] <= arena_base + arena_bytes, "arena"
            return start

        def place(name, shape, dt, offset):
            return nc.alloc_sbuf_tensor_at(name, shape, dt, offset=offset)

        h_hi = place("h_hi", [P, NB, NK, BLOCK], F32R, region(32 * KIB))
        h_lo_at = region(32 * KIB)
        h_lo = place("h_lo", [P, NB, NK, BLOCK], F32R, h_lo_at)
        raw = place("raw", [P, 2, D], F32, region(8 * KIB))
        w_hi = place("w_hi", [P, 4, D], F32R, region(16 * KIB))
        w_lo = place("w_lo", [P, 4, D], F32R, region(16 * KIB))
        x1_at = region(32 * KIB)
        x1 = place("x1", [P, NT, D], F32, x1_at)
        Y_at = region(32 * KIB)
        y = place("y", [P, NK, SPAN], F32, Y_at)
        mid_hi = [place(f"mid_hi{p}", [P, 2, SPAN], F32R, Y_at + p * 16 * KIB) for p in range(2)]
        mid_lo = [place(f"mid_lo{p}", [P, 2, SPAN], F32R, Y_at + (16 * p + 8) * KIB) for p in range(2)]
        YS_at = region(16 * KIB)
        y_hi = place("y_hi", [P, 2, 2, BLOCK], F32R, YS_at)
        y_lo = place("y_lo", [P, 2, 2, BLOCK], F32R, YS_at + 8 * KIB)
        us = place("us", [P, 2, SPAN + 8], F32, YS_at)
        gated = place("gated", [P, 2, BLOCK], F32, YS_at + 2 * (SPAN + 8) * 4)
        m_at = x1_at + 32 * KIB - (SPAN + 8) * 4
        m = place("m", [P, SPAN + 8], F32, m_at)
        ada_sum = place("ada_sum", [P, 2 * D], F32, x1_at + 16 * KIB)
        stage_y = place("stage_y", [P, TB, D], F32, Y_at + 16 * KIB)
        stage_h = place("stage_h", [P, TB, D], F32, h_lo_at + 16 * KIB)
        ada_tile = [place(f"ada_tile{i}", [P, 2 * D], F32, start + (i % 2) * 8 * KIB)
                    for i, start in enumerate((YS_at, YS_at, x1_at, x1_at,
                                               arena_base, arena_base, arena_base + 16 * KIB, arena_base + 16 * KIB))]
        gate_row = place("gate_row", [P, 2, D], F32, region(8 * KIB))
        scratch_at = region(4 * KIB)
        c_copy = place("c_copy", [P, NB, BLOCK], F32, scratch_at)
        square_out = place("square_out", [P, D], BF16, scratch_at)
        tmp = place("tmp", [P, BLOCK], F32, scratch_at + 2 * KIB)
        ident = place("ident", [P, P], F32, region(512))
        ones = place("ones", [P, P], F32, region(512))
        vec_rows = place("vec_rows", [P, 2, P], F32, region(1024))

        V_ADA, V_C = 0, 6 * NK
        V_GM, V_GF = V_C + NK, V_C + 2 * NK
        V_SC = V_GF + NK
        ROWS0 = V_SC + TAPS * NK
        V_FC, ROWS1 = ROWS0, TAPS * NF
        cols = place("cols", [P, ROWS0 + ROWS1], F32, region(4 * (ROWS0 + ROWS1)))
        cond = place("cond", [P, NK], F32, region(32))
        scale_c = place("scale_c", [P, 2, NK], F32, region(64))
        shift_c = place("shift_c", [P, 2, NK], F32, region(64))
        mod_tmp = place("mod_tmp", [P, NK], F32, region(32))
        sumsq = place("sumsq", [P, 4 * NT], F32, region(128))
        mean_sq = place("mean_sq", [P, 4 * NT], F32, region(128))
        rstd = place("rstd", [P, 4 * NT], F32, region(128))
        minus_half = place("minus_half", [P, 1], F32, region(32))
        m_halo = place("m_halo", [P, NK, 2], F32, region(NK * 8))
        u_halo = place("u_halo", [P, NF, 2], F32, region(NF * 8))

        ps = ctx.enter_context(nc.psum_tensor("ps", [P, 8, BLOCK], F32))

        def sem(name):
            return ctx.enter_context(nc.semaphore(name))

        vec_loaded, gate_bias_loaded = sem("vec_loaded"), sem("gate_bias_loaded")
        const_made, ident_zeroed = sem("const_made"), sem("ident_zeroed")
        vec_transposed, cols_made, cond_made = sem("vec_transposed"), sem("cols_made"), sem("cond_made")
        ada_loaded = [sem(f"ada_loaded{i}") for i in range(8)]
        ada_used, mod_reduced, mod_made = sem("ada_used"), sem("mod_reduced"), sem("mod_made")
        mod_step = sem("mod_step")
        raw_loaded = [sem(f"raw_loaded{i}") for i in range(2)]
        w_hi_made, w_ready, w_used, gate_folded = sem("w_hi_made"), sem("w_ready"), sem("w_used"), sem("gate_folded")
        load_turns, split_turns = sem("load_turns"), sem("split_turns")
        x_staged = [sem(f"x_staged{i}") for i in range(NT)]
        squared, rstd_made, rstd_step = sem("squared"), sem("rstd_made"), sem("rstd_step")
        normed, transposed = sem("normed"), sem("transposed")
        modulated, modulated_act = sem("modulated"), sem("modulated_act")
        h_hi_made, h_ready = sem("h_hi_made"), sem("h_ready")
        proj_done, c_copied, m_made = sem("proj_done"), sem("c_copied"), sem("m_made")
        m_tapped, conv_step, y_made = sem("m_tapped"), sem("conv_step"), sem("y_made")
        y_hi_made, y_split, y_used = sem("y_hi_made"), sem("y_split"), sem("y_used")
        mixer_done, mixer_scaled, x1_made = sem("mixer_done"), sem("mixer_scaled"), sem("x1_made")
        x1_loaded = [sem(f"x1_loaded{i}") for i in range(NB)]
        up_done, u_tapped, ffn_conv_step = sem("up_done"), sem("u_tapped"), sem("ffn_conv_step")
        convolved, silu_made, gated_made = sem("convolved"), sem("silu_made"), sem("gated_made")
        mid_hi_made, mid_ready = sem("mid_hi_made"), sem("mid_ready")
        down_done, down_added, out_stored = sem("down_done"), sem("down_added"), sem("out_stored")

        VECTORS = [("shift", 0), ("scale", 0), ("gate", 0), ("shift", 1), ("scale", 1), ("gate", 1)]
        PAIRS = 3

        def ada_place(p, k):
            return (k, 1) if p == 0 else (k % 4, 2 * p + k // 4)

        def tile_index(h, stage, t):
            return 2 * NT * h + NT * stage + t

        def stage_of(stage, t):
            return (stage_h if t < TB else stage_y)[:, t % TB, :]

        def banks_of(h, stage, t):
            if h == 0 and stage == 0:
                return 2 * (t if t < TB else t % 2)
            return (4 if stage == 1 and t >= TB else 0) + 2 * (t % 2)

        def sum_bank(v):
            return 6 + v if v < 2 else 2

        ITEMS = NF * NB
        DOWNS = 2 * NT
        NEXT_A = (0, 1, 2, 3, 5, 6, 7)
        block = ctx.enter_context(nc.Block())

        @block.sync
        def _(sp):
            def rows(dst, src):
                sp.dma_start(dst, src.rearrange("(r n) -> r n", n=P)).then_inc(vec_loaded, 16)

            def load_ada(p, ks):
                for k in ks:
                    i, _ = ada_place(p, k)
                    if p > 0:
                        sp.wait_ge(ada_used, NK * p + k - 3 if p > 1 or k >= 4 else NK)
                    sp.dma_start(ada_tile[i][:], ada_v[k][:, 2 * p * D:2 * (p + 1) * D]).then_inc(ada_loaded[i], 16)

            def load_raw(r, src, n):
                if not (isinstance(n, int) and n < 2):
                    sp.wait_ge(w_ready, n - 1)
                    sp.sem_inc(load_turns, 1)
                sp.dma_start(raw[:, r, :] if len(src.shape) == 2 else
                             raw[:, r, :].rearrange("p (a b) -> p a b", a=src.shape[1]),
                             src).then_inc(raw_loaded[r], 16)

            def sc_in_stripe(chunk, j):
                return sc_in_v[:, :, bass.ds(((j + 1) % 3) * D + chunk * P, P)]

            def up_stripe(chunk, j):
                return up_v[:, :, bass.ds(j * F + chunk * P, P)]

            def load_x(h, t):
                if h > 0 and t == 0:
                    sp.wait_ge(up_done, 2 * ITEMS * h)
                if h > 0 and t == TB:
                    sp.wait_ge(down_done, DOWNS * (GROUPS * h - 1))
                sp.dma_start(stage_of(0, t), x_t[NT * h + t]).then_inc(x_staged[t], 16)

            def load_b(U, pair):
                for j in range(6):
                    load_raw(j % 2, sc_in_stripe(2 * pair + j // 3, j % 3), U + 6 * pair + j)

            def load_residual(h, b):
                sp.dma_start(x1[:, TB * b:TB * b + TB, :],
                             x_t[NT * h + TB * b:NT * h + TB * b + TB].rearrange("t p d -> p t d")
                             ).then_inc(x1_loaded[b], 16)

            for h in range(HALVES):
                U = UNITS * h
                if h == 0:
                    rows(vec_rows[V_ADA:V_C, 0, :], ada_b[0])
                    rows(vec_rows[V_C:V_GM, 0, :], c[0])
                    rows(vec_rows[V_GM:V_GF, 0, :], ln_mix_g[0])
                    rows(vec_rows[V_GF:V_SC, 0, :], ln_ffn_g[0])
                    rows(vec_rows[V_SC:ROWS0, 0, :], sc_conv[0].rearrange("a n -> (a n)"))
                    rows(vec_rows[0:ROWS1, 1, :], ffn_conv[0].rearrange("a n -> (a n)"))
                    load_ada(0, range(NK))
                    load_raw(0, sc_in_stripe(0, 0), 0)
                    for t in range(TB, NT):
                        load_x(h, t)
                    load_raw(1, sc_in_stripe(0, 1), 1)
                    for i, v in enumerate((2, 5)):
                        sp.dma_start(gate_row[:, i, :], ada_b[:, v * D:(v + 1) * D].broadcast_to([P, D])).then_inc(gate_bias_loaded, 16)
                    load_raw(0, sc_in_stripe(0, 2), 2)
                    load_ada(1, range(4))
                    load_raw(1, sc_in_stripe(1, 0), 3)
                    load_raw(0, sc_in_stripe(1, 1), 4)
                    load_ada(1, range(4, 8))
                    load_raw(1, sc_in_stripe(1, 2), 5)
                    for j in range(6, 9):
                        load_raw(j % 2, sc_in_stripe(j // 3, j % 3), j)
                    load_ada(2, range(4))
                    for j in range(9, 12):
                        load_raw(j % 2, sc_in_stripe(j // 3, j % 3), j)
                    load_ada(2, range(4, 8))
                else:
                    for j in range(2, 6):
                        load_raw(j % 2, sc_in_stripe(j // 3, j % 3), U + j)
                with sp.Fori(2 if h == 0 else 1, NK // 2) as pair:
                    load_b(U, pair)
                if h == 0:
                    sp.wait_ge(mod_made, len(VECTORS))
                else:
                    sp.wait_ge(out_stored, 16 * NT * h)
                load_residual(h, 0)
                for i in range(UC):
                    dh, s = divmod(i, NK // 2)
                    load_raw(i % 2, sc_out_v[:, 2 * s:2 * s + 2, dh * BLOCK:(dh + 1) * BLOCK], U + C0 + i)
                    if i == 4:
                        sp.wait_ge(y_made, NK * NB * (h + 1))
                        load_residual(h, 1)
                for i in range(UP):
                    load_raw(i % 2, up_stripe(i // 2, i % 2), U + P0 + i)
                with sp.Fori(0, (GROUPS - 1) // 2) as g2:
                    for e in range(2):
                        for i in range(4):
                            load_raw(i % 2, up_stripe(4 * g2 + 2 * e + 2 + i // 2, i % 2),
                                     U + E0 + 12 * g2 + 6 * e + i)
                        for i in range(2):
                            load_raw(i % 2, down_v[:, bass.ds(4 * g2 + 2 * e + i, 1), :],
                                     U + E0 + 12 * g2 + 6 * e + 4 + i)
                for i in range(2):
                    load_raw(i % 2, down_v[:, 2 * (GROUPS - 1) + i, :], U + L0 + i)
                if h + 1 < HALVES:
                    for t in range(TB):
                        load_x(h + 1, t)
                    load_raw(0, sc_in_stripe(0, 0), U + UNITS)
                    load_raw(1, sc_in_stripe(0, 1), U + UNITS + 1)
                    for t in range(TB, NT):
                        load_x(h + 1, t)
                for t in range(NT):
                    sp.wait_ge(down_added, DOWNS * (GROUPS * (h + 1) - 1) + 2 * t + 2 + 4)
                    sp.dma_start(out_t[NT * h + t], x1[:, t, :]).then_inc(out_stored, 16)
            sp.wait_ge(out_stored, 16 * NT * HALVES)

        @block.gpsimd
        def _(pool):
            pool.memset(ident[:], 0.0).then_inc(ident_zeroed, 1)
            pool.memset(ones[:], 1.0)
            pool.memset(minus_half[:], -0.5)
            pool.memset(m_halo[:], 0.0)
            pool.memset(u_halo[:], 0.0)
            pool.wait_ge(ident_zeroed, 1)
            pool.affine_select(out=ident[:], in_=ident[:], compare_op=ALU.not_equal, fill=1.0,
                               base=0, pattern=[[-1, P]], channel_multiplier=1).then_inc(const_made, 1)
            def split(n, n2, slot, used, gate=None):
                r, m = n2
                pool.wait_ge(raw_loaded[r], 16 * (m + 1))
                if used is not None:
                    pool.wait_ge(w_used, used)
                if gate is not None:
                    pool.tensor_tensor(raw[:, r, :], raw[:, r, :], gate_row[:, 1, :], ALU.mult).then_inc(gate_folded, 1)
                    pool.wait_ge(gate_folded, gate)
                pool.sem_inc(split_turns, 1)
                pool.tensor_scalar(w_hi[:, slot, :], raw[:, r, :], 1.0, 1.0, ALU.mult, ALU.mult).then_inc(w_hi_made, 1)
                pool.wait_ge(w_hi_made, n + 1)
                pool.tensor_tensor(w_lo[:, slot, :], raw[:, r, :], w_hi[:, slot, :].bitcast(F32),
                                   ALU.subtract).then_inc(w_ready, 1)

            def take_rstd(h, stage, t):
                i = tile_index(h, stage, t)
                pool.wait_ge(squared, i + 1)
                pool.tensor_scalar(mean_sq[:, i:i + 1], sumsq[:, i:i + 1], 1.0 / D, RMS_EPS,
                                   ALU.mult, ALU.add).then_inc(rstd_step, 1)
                pool.wait_ge(rstd_step, i + 1)
                pool.tensor_tensor(rstd[:, i:i + 1], mean_sq[:, i:i + 1], minus_half[:], ALU.pow).then_inc(rstd_made, 1)

            def make_h_lo(h, stage, t):
                i = tile_index(h, stage, t)
                b, tt = divmod(t, TB)
                cut = slice(tt * P, tt * P + P)
                pool.wait_ge(h_hi_made, i + 1)
                if t >= TB:
                    pool.wait_ge(h_ready, i)
                pool.tensor_tensor(h_lo[:, b, :, cut], stage_of(stage, t).rearrange("p (k n) -> p k n", k=NK),
                                   h_hi[:, b, :, cut].bitcast(F32), ALU.subtract).then_inc(h_ready, 1)

            def split_at(U, i, extra=0, extra_raw=0, gate=None):
                o = occupant_of(i)
                used = None if U + o < 0 else U + o + 1 + extra
                split(U + i + extra, (i % 2, (U + i) // 2 + extra_raw), slot_of(i), used, gate)

            for h in range(HALVES):
                U = UNITS * h
                for t in range(TB):
                    take_rstd(h, 0, t)
                split_at(U, 0)
                split_at(U, 1)
                if h == 0:
                    for t in range(TB, NT):
                        take_rstd(h, 0, t)
                for t in range(TB):
                    make_h_lo(h, 0, t)
                    if h > 0:
                        take_rstd(h, 0, TB + t)
                for t in range(TB, NT):
                    make_h_lo(h, 0, t)
                for i in range(2, 6):
                    split_at(U, i)
                with pool.Fori(0, NK // 2 - 1) as pair:
                    for i in range(6, 12):
                        split_at(U, i, 6 * pair, 3 * pair)
                for i in range(C0, P0):
                    split_at(U, i)
                take_rstd(h, 1, 0)
                take_rstd(h, 1, 1)
                split_at(U, P0)
                take_rstd(h, 1, 2)
                take_rstd(h, 1, 3)
                for t in range(TB):
                    make_h_lo(h, 1, t)
                split_at(U, P0 + 1)
                take_rstd(h, 1, TB)
                take_rstd(h, 1, TB + 1)
                split_at(U, P0 + 2)
                take_rstd(h, 1, TB + 2)
                take_rstd(h, 1, TB + 3)
                make_h_lo(h, 1, TB)
                split_at(U, P0 + 3)
                for t in range(TB + 1, NT):
                    make_h_lo(h, 1, t)
                if h == 0:
                    pool.wait_ge(mod_made, len(VECTORS))
                folded = 2 * GROUPS * h
                with pool.Fori(0, (GROUPS - 1) // 2) as g2:
                    for j in range(12):
                        e, i = divmod(j, 6)
                        split_at(U, E0 + j, 12 * g2, 6 * g2,
                                 gate=folded + 4 * g2 + 2 * e + i - 4 + 1 if i >= 4 else None)
                for i in range(2):
                    split_at(U, L0 + i, gate=folded + 2 * (GROUPS - 1) + i + 1)

        @block.scalar
        def _(act):
            def square(h, stage, t):
                i = tile_index(h, stage, t)
                if stage == 0:
                    act.wait_ge(x_staged[t], 16 * (h + 1))
                    src = stage_of(stage, t)
                else:
                    act.wait_ge(x1_made, 2 * NT * h + NT + t + 1)
                    src = x1[:, t, :]
                if i > 0:
                    act.wait_ge(squared, i)
                act.activation(square_out[:], src, ACT.Square, accum_out=sumsq[:, i:i + 1]).then_inc(squared, 1)

            def norm(h, stage, t):
                i = tile_index(h, stage, t)
                act.wait_ge(rstd_made, i + 1)
                src = stage_of(stage, t) if stage == 0 else x1[:, t, :]
                act.activation(stage_of(stage, t), src, ACT.Copy, scale=rstd[:, i:i + 1]).then_inc(normed, 1)

            def modulate(h, stage, t):
                i = tile_index(h, stage, t)
                bank = banks_of(h, stage, t)
                dst = stage_of(stage, t)
                act.wait_ge(transposed, i + 1)
                for k in range(NK // 2, NK):
                    op = act.activation(dst[:, k * P:(k + 1) * P], ps[:, bank + 1, (k % 4) * P:(k % 4 + 1) * P],
                                        ACT.Identity, scale=scale_c[:, stage, k:k + 1], bias=shift_c[:, stage, k:k + 1])
                op.then_inc(modulated_act, 1)

            def stage_b(h, chunk):
                N = NB * NK * h
                for b in range(NB):
                    act.wait_ge(proj_done, 6 * NK * h + 6 * chunk + b + 1)
                    act.activation(c_copy[:, b, :], ps[:, 4 + b, :], ACT.Copy).then_inc(c_copied, 1)
                for b in range(NB):
                    act.wait_ge(m_made, N + NB * chunk + b + 1)
                    act.activation(y[:, bass.ds(chunk, 1), b * BLOCK:(b + 1) * BLOCK],
                                   m[:, 2 + b * BLOCK:2 + (b + 1) * BLOCK].unsqueeze(1), ACT.Copy,
                                   scale=cols[:, bass.ds(V_SC + 2 * NK + chunk, 1)]).then_inc(m_tapped, 1)

            def make_y_hi(h, n):
                dh, grp, s = n // 8, n // 4 % 2, n % 4
                if n < 2:
                    act.wait_ge(y_made, NB * (NK * h + NK - 1))
                elif n == 3:
                    act.wait_ge(y_made, NB * NK * (h + 1) - 1)
                elif n == 4:
                    act.wait_ge(y_made, NB * NK * (h + 1))
                if n >= 2:
                    act.wait_ge(y_used, 15 * h + n - 1)
                act.activation(y_hi[:, n % 2], y[:, 2 * s:2 * s + 2, grp * BLOCK:(grp + 1) * BLOCK],
                               ACT.Copy).then_inc(y_hi_made, 1)

            def ffn_item(h, q, qe, chunk, chunk_e, b, par, j):
                Q = ITEMS * h + q + qe
                pp = q % 2
                u_bank, ce = 2 * pp, chunk + chunk_e
                act.wait_ge(up_done, 2 * Q + 1)
                if b == 0:
                    act.activation(us[:, j, 0:2], u_halo[:, bass.ds(ce, 1), :].rearrange("p a b -> p (a b)"), ACT.Copy)
                act.activation(us[:, j, 2 + b * BLOCK:2 + (b + 1) * BLOCK], ps[:, u_bank, :], ACT.Copy)
                if b == NB - 1 and h + 1 < HALVES:
                    act.activation(u_halo[:, bass.ds(ce, 1), :].rearrange("p a b -> p (a b)"),
                                   ps[:, u_bank, BLOCK - 2:BLOCK], ACT.Copy)
                act.activation(gated[:, pp, :], ps[:, u_bank, :], ACT.Copy,
                               scale=cols[:, bass.ds(V_FC + 2 * NF + ce, 1)]).then_inc(u_tapped, 1)
                act.wait_ge(convolved, Q + 1)
                act.activation(gated[:, pp, :], gated[:, pp, :], ACT.Silu).then_inc(silu_made, 1)
                act.wait_ge(gated_made, Q + 1)
                act.activation(mid_hi[par][:, j, b * BLOCK:(b + 1) * BLOCK], gated[:, pp, :], ACT.Copy).then_inc(mid_hi_made, 1)

            for t in range(TB):
                act.dma_start(stage_of(0, t), x_t[t]).then_inc(x_staged[t], 16)
            act.wait_ge(const_made, 1)
            act.wait_ge(cols_made, 1)
            act.activation(cond[:], cols[:, V_C:V_GM], ACT.Silu).then_inc(cond_made, 1)

            def norm_block(h, stage, t0):
                square(h, stage, t0)
                for t in range(t0 + 1, t0 + TB):
                    square(h, stage, t)
                    norm(h, stage, t - 1)
                norm(h, stage, t0 + TB - 1)

            norm_block(0, 0, 0)
            act.wait_ge(mod_made, 2)
            for t in range(TB):
                modulate(0, 0, t)
            norm_block(0, 0, TB)
            for t in range(TB, NT):
                modulate(0, 0, t)
            for h in range(HALVES):
                with act.Fori(0, NK) as chunk:
                    stage_b(h, chunk)
                for n in range(14):
                    make_y_hi(h, n)
                square(h, 1, 0)
                square(h, 1, 1)
                norm(h, 1, 0)
                make_y_hi(h, 14)
                norm(h, 1, 1)
                square(h, 1, 2)
                square(h, 1, 3)
                norm(h, 1, 2)
                make_y_hi(h, 15)
                norm(h, 1, 3)
                for t in range(TB):
                    modulate(h, 1, t)
                norm_block(h, 1, TB)
                modulate(h, 1, TB)
                modulate(h, 1, TB + 1)
                ffn_item(h, 0, 0, 0, 0, 0, 0, 0)
                modulate(h, 1, TB + 2)
                modulate(h, 1, TB + 3)
                ffn_item(h, 1, 0, 1, 0, 0, 0, 1)
                ffn_item(h, 2, 0, 0, 0, 1, 0, 0)
                ffn_item(h, 3, 0, 1, 0, 1, 0, 1)
                with act.Fori(0, (GROUPS - 1) // 2) as g2:
                    for e in range(2):
                        for i in range(4):
                            ffn_item(h, 4 + 4 * e + i, 8 * g2, 2 + 2 * e + i // 2, 4 * g2, i % 2, 1 - e, i // 2)

                if h + 1 < HALVES:
                    norm_block(h + 1, 0, 0)
                    modulate(h + 1, 0, 0)
                    square(h + 1, 0, TB)
                    for t in range(1, TB):
                        modulate(h + 1, 0, t)
                        norm(h + 1, 0, TB + t - 1)
                        square(h + 1, 0, TB + t)
                    norm(h + 1, 0, NT - 1)
                    for t in range(TB, NT):
                        modulate(h + 1, 0, t)

        @block.vector
        def _(dve):
            def ada_products(p, ks):
                for k in ks:
                    i, m = ada_place(p, k)
                    dve.wait_ge(ada_loaded[i], 16 * m)
                    if k == 0:
                        if p > 0:
                            dve.wait_ge(mod_reduced, 2 * p)
                        dve.tensor_scalar(ada_sum[:], ada_tile[i][:], cond[:, k:k + 1], None, ALU.mult).then_inc(ada_used, 1)
                    else:
                        dve.wait_ge(ada_used, NK * p + k)
                        dve.scalar_tensor_tensor(out=ada_sum[:], in0=ada_tile[i][:], scalar=cond[:, k:k + 1],
                                                 in1=ada_sum[:], op0=ALU.mult, op1=ALU.add).then_inc(ada_used, 1)

            def mod_vector(v):
                kind, which = VECTORS[v]
                bias = cols[:, V_ADA + v * NK:V_ADA + (v + 1) * NK]
                dve.wait_ge(mod_reduced, v + 1)
                if kind == "gate":
                    dve.wait_ge(gate_bias_loaded, 32)
                    dve.tensor_tensor(gate_row[:, which, 0:BLOCK], ps[:, sum_bank(v), :], gate_row[:, which, 0:BLOCK], ALU.add)
                    dve.tensor_tensor(gate_row[:, which, BLOCK:D], ps[:, sum_bank(v) + 1, :], gate_row[:, which, BLOCK:D],
                                      ALU.add).then_inc(mod_made, 1)
                elif kind == "shift":
                    dve.tensor_tensor(shift_c[:, which, :], ps[:, sum_bank(v), 0:NK], bias, ALU.add).then_inc(mod_made, 1)
                else:
                    gain = cols[:, V_GF:V_SC] if which else cols[:, V_GM:V_GF]
                    dve.tensor_tensor(mod_tmp[:], ps[:, sum_bank(v), 0:NK], bias, ALU.add).then_inc(mod_step, 1)
                    dve.wait_ge(mod_step, which + 1)
                    dve.scalar_tensor_tensor(out=scale_c[:, which, :], in0=mod_tmp[:], scalar=1.0, in1=gain,
                                             op0=ALU.add, op1=ALU.mult).then_inc(mod_made, 1)

            def modulate(h, stage, t):
                i = tile_index(h, stage, t)
                bank = banks_of(h, stage, t)
                dst = stage_of(stage, t)
                dve.wait_ge(transposed, i + 1)
                for k in range(NK // 2):
                    op = dve.tensor_scalar(dst[:, k * P:(k + 1) * P],
                                           ps[:, bank + k // 4, (k % 4) * P:(k % 4 + 1) * P],
                                           scale_c[:, stage, k:k + 1], shift_c[:, stage, k:k + 1], ALU.mult, ALU.add)
                op.then_inc(modulated, 1)
                b, tt = divmod(t, TB)
                dve.wait_ge(modulated, i + 1)
                dve.wait_ge(modulated_act, i + 1)
                dve.tensor_copy(h_hi[:, b, :, tt * P:tt * P + P],
                                dst.rearrange("p (k n) -> p k n", k=NK)).then_inc(h_hi_made, 1)

            def stage_b(h, chunk, last=False):
                N = NB * NK * h

                def tap(w):
                    return cols[:, bass.ds(V_SC + w * NK + chunk, 1)]

                def yb(b):
                    return y[:, bass.ds(chunk, 1), b * BLOCK:(b + 1) * BLOCK].rearrange("p a n -> p (a n)")

                halo = m_halo[:, bass.ds(chunk, 1), :].rearrange("p a n -> p (a n)")
                dve.tensor_copy(m[:, 0:2], halo)
                for b in range(NB):
                    dve.wait_ge(c_copied, N + NB * chunk + b + 1)
                    dve.wait_ge(proj_done, 6 * NK * h + 6 * chunk + NB + b + 1)
                    dve.tensor_tensor(m[:, 2 + b * BLOCK:2 + (b + 1) * BLOCK], ps[:, 6 + b, :], c_copy[:, b, :],
                                      ALU.mult).then_inc(m_made, 1)
                for b in range(NB):
                    dve.wait_ge(m_tapped, N + NB * chunk + b + 1)
                    dve.scalar_tensor_tensor(out=yb(b), in0=m[:, 1 + b * BLOCK:1 + (b + 1) * BLOCK], scalar=tap(1),
                                             in1=yb(b), op0=ALU.mult, op1=ALU.add).then_inc(conv_step, 1)
                if h + 1 < HALVES:
                    dve.tensor_copy(halo, m[:, SPAN:SPAN + 2])
                for b in range(NB):
                    dve.wait_ge(conv_step, 2 * N + 2 * NB * chunk + b + 1)
                    dve.scalar_tensor_tensor(out=yb(b), in0=m[:, b * BLOCK:(b + 1) * BLOCK], scalar=tap(0),
                                             in1=yb(b), op0=ALU.mult, op1=ALU.add).then_inc(conv_step, 1)
                if last:
                    make_y_lo(h, 0)
                    make_y_lo(h, 1)
                for b in range(NB):
                    dve.wait_ge(conv_step, 2 * N + 2 * NB * chunk + NB + b + 1)
                    dve.wait_ge(proj_done, 6 * NK * h + 6 * chunk + 2 * NB + b + 1)
                    dve.tensor_tensor(yb(b), ps[:, b, :], yb(b), ALU.mult).then_inc(y_made, 1)

            def make_y_lo(h, n):
                grp, s = n // 4 % 2, n % 4
                dve.wait_ge(y_hi_made, 16 * h + n + 1)
                dve.tensor_tensor(y_lo[:, n % 2], y[:, 2 * s:2 * s + 2, grp * BLOCK:(grp + 1) * BLOCK],
                                  y_hi[:, n % 2].bitcast(F32), ALU.subtract).then_inc(y_split, 1)

            def residual(h, group):
                dh, grp = divmod(group, 2)
                cut = slice(dh * BLOCK, (dh + 1) * BLOCK)
                if h == 0 and group == 0:
                    dve.wait_ge(mod_made, len(VECTORS))
                if dh == 0:
                    dve.wait_ge(x1_loaded[grp], 16 * (h + 1))
                for i in range(TB):
                    n = 16 * h + 4 * group + i
                    t = TB * grp + i
                    dve.wait_ge(mixer_done, n + 1)
                    if n > 0:
                        dve.wait_ge(x1_made, n)
                    dve.tensor_tensor(tmp[:], ps[:, 4 + i, :], gate_row[:, 0, cut], ALU.mult).then_inc(mixer_scaled, 1)
                    dve.wait_ge(mixer_scaled, n + 1)
                    dve.tensor_tensor(x1[:, t, cut], tmp[:], x1[:, t, cut], ALU.add).then_inc(x1_made, 1)

            def ffn_item(h, q, qe, chunk, chunk_e, b, par, j):
                Q = ITEMS * h + q + qe
                pp = q % 2
                ce = chunk + chunk_e
                g = gated[:, pp, :]

                def tap(w):
                    return cols[:, bass.ds(V_FC + w * NF + ce, 1)]

                dve.wait_ge(u_tapped, Q + 1)
                dve.scalar_tensor_tensor(out=g, in0=us[:, j, 1 + b * BLOCK:1 + (b + 1) * BLOCK], scalar=tap(1),
                                         in1=g, op0=ALU.mult, op1=ALU.add).then_inc(ffn_conv_step, 1)
                dve.wait_ge(ffn_conv_step, Q + 1)
                dve.scalar_tensor_tensor(out=g, in0=us[:, j, b * BLOCK:(b + 1) * BLOCK], scalar=tap(0),
                                         in1=g, op0=ALU.mult, op1=ALU.add).then_inc(convolved, 1)
                dve.wait_ge(silu_made, Q + 1)
                dve.wait_ge(up_done, 2 * Q + 2)
                dve.tensor_tensor(g, ps[:, 2 * pp + 1, :], g, ALU.mult).then_inc(gated_made, 1)
                dve.wait_ge(mid_hi_made, Q + 1)
                cut = slice(b * BLOCK, (b + 1) * BLOCK)
                dve.tensor_tensor(mid_lo[par][:, j, cut], g, mid_hi[par][:, j, cut].bitcast(F32),
                                  ALU.subtract).then_inc(mid_ready, 1)

            def add_down(h, g, ge, next_a=False):
                N = DOWNS * (GROUPS * h + g + ge)
                for r in range(DOWNS):
                    t, dh = divmod(r, 2)
                    cut = slice(dh * BLOCK, (dh + 1) * BLOCK)
                    dve.wait_ge(down_done, N + r + 1)
                    dve.tensor_tensor(x1[:, t, cut], ps[:, 4 + r % 4, :], x1[:, t, cut], ALU.add).then_inc(down_added, 1)
                    if next_a and dh == 1 and t in NEXT_A:
                        modulate(h + 1, 0, NEXT_A.index(t))

            dve.sem_inc(down_added, 4)
            dve.wait_ge(const_made, 1)
            dve.wait_ge(vec_transposed, 1)
            dve.tensor_copy(cols[:], ps[:, 2, 0:ROWS0 + ROWS1]).then_inc(cols_made, 1)
            dve.wait_ge(cond_made, 1)
            ada_products(0, range(NK))
            mod_vector(0)
            mod_vector(1)
            dve.wait_ge(mod_made, 2)
            for t in range(NT):
                modulate(0, 0, t)
            for h in range(HALVES):
                if h == 0:
                    for chunk in range(4):
                        p, part = 1 + chunk // 2, chunk % 2
                        ada_products(p, range(4 * part, 4 * part + 4))
                        stage_b(h, chunk)
                        if part == 1:
                            mod_vector(2 * p)
                            mod_vector(2 * p + 1)
                    with dve.Fori(4, NK - 1) as chunk:
                        stage_b(h, chunk)
                else:
                    dve.wait_ge(out_stored, 16 * NT * h)
                    with dve.Fori(0, NK - 1) as chunk:
                        stage_b(h, chunk)
                stage_b(h, NK - 1, last=True)
                for n in range(2, 16):
                    make_y_lo(h, n)
                    if n % 4 == 0 and n > 0:
                        residual(h, n // 4 - 1)
                for t in range(TB):
                    modulate(h, 1, t)
                residual(h, 3)
                modulate(h, 1, TB)
                modulate(h, 1, TB + 1)
                ffn_item(h, 0, 0, 0, 0, 0, 0, 0)
                modulate(h, 1, TB + 2)
                modulate(h, 1, TB + 3)
                ffn_item(h, 1, 0, 1, 0, 0, 0, 1)
                ffn_item(h, 2, 0, 0, 0, 1, 0, 0)
                ffn_item(h, 3, 0, 1, 0, 1, 0, 1)
                with dve.Fori(0, (GROUPS - 1) // 2) as g2:
                    for e in range(2):
                        for i in range(4):
                            ffn_item(h, 4 + 4 * e + i, 8 * g2, 2 + 2 * e + i // 2, 4 * g2, i % 2, 1 - e, i // 2)
                        add_down(h, e, 2 * g2)
                add_down(h, GROUPS - 1, 0, h + 1 < HALVES)
                if h + 1 < HALVES:
                    for t in range(len(NEXT_A), NT):
                        modulate(h + 1, 0, t)

        @block.tensor
        def _(pe):
            def products(bank, pairs, start=True, stop=True, gone=(), first_done=None):
                last = len(pairs) - 1
                gone = list(gone)
                for i, ((s_hi, s_lo), (v_hi, v_lo)) in enumerate(pairs):
                    a = pe.matmul(ps[:, bank, :], s_hi, v_hi, start=start and i == 0, stop=False)
                    b = pe.matmul(ps[:, bank, :], s_hi, v_lo, start=False, stop=False)
                    op = pe.matmul(ps[:, bank, :], s_lo, v_hi, start=False, stop=stop and i == last)
                    if i == 0:
                        for done, signal in zip((a, b), gone):
                            done.then_inc(signal, 1)
                        if first_done is not None:
                            op.then_inc(first_done, 1)
                return op

            def project(slot, b, bank, gone=()):
                return products(bank, [((w_hi[:, slot, k * P:(k + 1) * P], w_lo[:, slot, k * P:(k + 1) * P]),
                                        (h_hi[:, b, k, :], h_lo[:, b, k, :])) for k in range(NK)], gone=gone)

            def transpose_tile(h, stage, t):
                i = tile_index(h, stage, t)
                bank = banks_of(h, stage, t)
                src = stage_of(stage, t)
                pe.wait_ge(normed, i + 1)
                if h == 0 and stage == 0 and t == 3:
                    pe.wait_ge(mod_made, 2)
                if stage == 1 and t == TB:
                    pe.wait_ge(x1_made, 16 * h + 16)
                before = [u for u in range(t) if banks_of(h, stage, u) == bank]
                if before:
                    pe.wait_ge(modulated, tile_index(h, stage, before[-1]) + 1)
                    pe.wait_ge(modulated_act, tile_index(h, stage, before[-1]) + 1)
                for k in range(NK):
                    op = pe.transpose(ps[:, bank + k // 4, (k % 4) * P:(k % 4 + 1) * P],
                                      src[:, k * P:(k + 1) * P], ident[:])
                op.then_inc(transposed, 1)

            def reduce_mod(v):
                part = ada_sum[:, v % 2 * D:(v % 2 + 1) * D]
                pe.wait_ge(ada_used, NK * (v // 2 + 1))
                if v > 2:
                    pe.wait_ge(mod_made, v)
                if VECTORS[v][0] == "gate":
                    for i in range(2):
                        op = pe.matmul(ps[:, sum_bank(v) + i, :], ones[:], part[:, i * BLOCK:(i + 1) * BLOCK],
                                       start=True, stop=True)
                else:
                    for k in range(NK):
                        op = pe.matmul(ps[:, sum_bank(v), k:k + 1], part[:, k * P:(k + 1) * P], ones[:, 0:1],
                                       start=True, stop=True)
                op.then_inc(mod_reduced, 1)

            def stage_b(h, chunk, first=False):
                N = NB * NK * h
                free = (c_copied, m_made, y_made)
                for j in range(3):
                    pe.wait_ge(w_ready, UNITS * h + 3 * chunk + j + 1)
                    for b in range(NB):
                        if first and j == 0:
                            pe.wait_ge(h_ready, tile_index(h, 0, TB * b + TB - 1) + 1)
                            if h > 0 and b == 0:
                                pe.wait_ge(down_added, DOWNS * GROUPS * h + 4)
                        if not first:
                            pe.wait_ge(free[j], N + NB * (chunk - 1) + b + 1)
                        gone = (w_used,) if b == 0 and not (first and j == 0 and h == 0) else ()
                        project(j, b, (4, 6, 0)[j] + b, gone).then_inc(proj_done, 1)

            def mixer_step(h, n):
                dh, grp, s = n // 8, n // 4 % 2, n % 4
                slot = slot_of(C0 + 4 * dh + s)
                gone = [y_used] if n > 0 else [w_used]
                if n > 0 and (n - 1) // 4 % 2 == 1:
                    gone.append(w_used)
                if grp == 0:
                    pe.wait_ge(w_ready, UNITS * h + C0 + 4 * dh + s + 1)
                pe.wait_ge(y_split, 16 * h + n + 1)
                for i in range(TB):
                    if s == 0 and n > 0:
                        pe.wait_ge(x1_made, 16 * h + n - TB + i + 1)
                    cut = slice(i * P, (i + 1) * P)
                    op = products(4 + i, [((y_hi[:, n % 2, kk, cut], y_lo[:, n % 2, kk, cut]),
                                           (w_hi[:, slot, kk * BLOCK:(kk + 1) * BLOCK],
                                            w_lo[:, slot, kk * BLOCK:(kk + 1) * BLOCK])) for kk in range(2)],
                                  s == 0, s == 3, gone if i == 0 else ())
                    if s == 3:
                        op.then_inc(mixer_done, 1)

            def up_part(h, q, qe, i, ie, j, b, gone):
                if j == 0 and q >= 2:
                    pe.wait_ge(gated_made, ITEMS * h + q + qe - 1)
                if b == 0:
                    pe.wait_ge(w_ready, UNITS * h + i + ie + 1)
                project(slot_of(i), b, 2 * (q % 2) + j, (w_used,) if gone else ()).then_inc(up_done, 1)

            def down(h, g, ge, i, ie, par, next_a=False):
                N = DOWNS * (GROUPS * h + g + ge)
                slots = slot_of(i), slot_of(i + 1)
                pe.wait_ge(w_ready, UNITS * h + i + ie + 2)
                pe.wait_ge(mid_ready, ITEMS * h + 4 * (g + ge) + 4)
                for r in range(DOWNS):
                    t, dh = divmod(r, 2)
                    cut = slice(t * P, (t + 1) * P)
                    pe.wait_ge(down_added, N + r + 1)
                    products(4 + r % 4, [((mid_hi[par][:, j, cut], mid_lo[par][:, j, cut]),
                                          (w_hi[:, slots[j], dh * BLOCK:(dh + 1) * BLOCK],
                                           w_lo[:, slots[j], dh * BLOCK:(dh + 1) * BLOCK])) for j in range(2)],
                             gone=(w_used,) if r == 0 else (),
                             first_done=w_used if r == DOWNS - 1 else None).then_inc(down_done, 1)
                    if next_a and dh == 1 and t in NEXT_A:
                        if t == NEXT_A[0]:
                            pe.wait_ge(gated_made, ITEMS * (h + 1))
                        transpose_tile(h + 1, 0, NEXT_A.index(t))

            pe.wait_ge(const_made, 1)
            pe.wait_ge(vec_loaded, 16 * 6)
            pe.transpose(ps[:, 2, 0:ROWS0], vec_rows[0:ROWS0, 0, :], ident[0:ROWS0, 0:ROWS0])
            pe.transpose(ps[:, 2, ROWS0:ROWS0 + ROWS1], vec_rows[0:ROWS1, 1, :], ident[0:ROWS1, 0:ROWS1]
                         ).then_inc(vec_transposed, 1)
            pe.wait_ge(cols_made, 1)
            for t in range(3):
                transpose_tile(0, 0, t)
            reduce_mod(0)
            reduce_mod(1)
            for t in range(3, NT):
                transpose_tile(0, 0, t)
            for h in range(HALVES):
                if h == 0:
                    for chunk in range(4):
                        stage_b(h, chunk, chunk == 0)
                        if chunk % 2 == 1:
                            reduce_mod(chunk + 1)
                            reduce_mod(chunk + 2)
                    with pe.Fori(4, NK) as chunk:
                        stage_b(h, chunk)
                else:
                    stage_b(h, 0, True)
                    with pe.Fori(1, NK) as chunk:
                        stage_b(h, chunk)
                for n in range(14):
                    mixer_step(h, n)
                transpose_tile(h, 1, 0)
                transpose_tile(h, 1, 1)
                mixer_step(h, 14)
                transpose_tile(h, 1, 2)
                transpose_tile(h, 1, 3)
                mixer_step(h, 15)
                pe.wait_ge(h_ready, tile_index(h, 1, TB - 1) + 1)
                up_part(h, 0, 0, P0, 0, 0, 0, True)
                transpose_tile(h, 1, TB)
                up_part(h, 0, 0, P0 + 1, 0, 1, 0, False)
                transpose_tile(h, 1, TB + 1)
                transpose_tile(h, 1, TB + 2)
                up_part(h, 1, 0, P0 + 2, 0, 0, 0, False)
                transpose_tile(h, 1, TB + 3)
                up_part(h, 1, 0, P0 + 3, 0, 1, 0, False)
                pe.wait_ge(h_ready, tile_index(h, 1, NT - 1) + 1)
                for i in range(4):
                    up_part(h, 2 + i // 2, 0, P0 + i, 0, i % 2, 1, i > 0)
                with pe.Fori(0, (GROUPS - 1) // 2) as g2:
                    for e in range(2):
                        for i in range(4):
                            b = i % 2
                            unit = E0 + 6 * e + 2 * (i // 2)
                            up_part(h, 4 + 4 * e + i, 8 * g2, unit, 12 * g2, 0, b, b == 0)
                            up_part(h, 4 + 4 * e + i, 8 * g2, unit + 1, 12 * g2, 1, b, b == 1)
                        down(h, e, 2 * g2, E0 + 6 * e + 4, 12 * g2, e)
                down(h, GROUPS - 1, 0, L0, 0, 0, h + 1 < HALVES)
                if h + 1 < HALVES:
                    for t in range(len(NEXT_A), NT):
                        transpose_tile(h + 1, 0, t)


_INS = ['x', 'c', 'ln_mix_g', 'ln_ffn_g', 'ada_w', 'ada_b', 'ffn_up', 'ffn_conv', 'ffn_down', 'sc_in', 'sc_conv', 'sc_out']


def kernel(**inputs):
    import numpy as _np
    import concourse.bacc as _bacc
    from concourse import mybir as _mybir
    from concourse.bass_utils import run_bass_kernel_spmd as _run

    nc = _bacc.Bacc("TRN2", target_bir_lowering=False, num_devices=1)
    arrays, args = {}, []
    for name in _INS:
        a = _np.ascontiguousarray(inputs[name])
        arrays[f"in_{name}_dram"] = a
        args.append(nc.dram_tensor(f"in_{name}_dram", a.shape, _mybir.dt.from_np(a.dtype), kind="ExternalInput").ap())
    shape = inputs["x"].shape
    args.append(nc.dram_tensor("out_0_dram", shape, _mybir.dt.float32, kind="ExternalOutput").ap())
    decoder_layer(nc, *args)
    r = _run(nc, [arrays], core_ids=[0])
    return r.results[0]["out_0_dram"]
```

```python
from contextlib import ExitStack

import concourse.bass as bass
from concourse import mybir

F32 = mybir.dt.float32
F32R = mybir.dt.float32r
BF16 = mybir.dt.bfloat16
ALU = mybir.AluOpType
ACT = mybir.ActivationFunctionType

P = 128
RMS_EPS = 1e-6
HALVES = 2
BLOCK = 512
KIB = 1024


def decoder_layer(nc, x, c, ln_mix_g, ln_ffn_g, ada_w, ada_b, ffn_up, ffn_conv, ffn_down,
                  sc_in, sc_conv, sc_out, out):
    _, SEQ, D = x.shape
    F = ffn_down.shape[1]
    SPAN = SEQ // HALVES
    NK = D // P
    NF = F // P
    NB = SPAN // BLOCK
    NT = SPAN // P
    TB = BLOCK // P
    GROUPS = NF // 2
    TAPS = 3
    assert NB == 2 and NK == 8 and D == 2 * BLOCK and NF % 2 == 0 and GROUPS % 2 == 1

    UB = 3 * NK
    UC = 2 * (NK // 2)
    UP = 4
    UE = 6 * (GROUPS - 1)
    UNITS = UB + UC + UP + UE + 2
    C0, P0, E0, L0 = UB, UB + UC, UB + UC + UP, UB + UC + UP + UE
    assert UNITS % 2 == 0 and UB % 6 == 0

    def slot_of(i):
        if i < C0:
            return (1, 0, 2)[i % 3]
        return (3, 1, 0, 2)[(i - C0) % 4] if i < E0 else (3, 2, 1, 0)[(i - E0) % 4]

    def occupant_of(i):
        j = i - 1
        while slot_of(j % UNITS) != slot_of(i):
            j -= 1
        return j

    x_t = x[0].rearrange("(t p) d -> t p d", p=P)
    out_t = out[0].rearrange("(t p) d -> t p d", p=P)
    sc_in_v = sc_in[0].rearrange("(k p) n -> p k n", p=P)
    up_v = ffn_up[0].rearrange("(k p) n -> p k n", p=P)
    sc_out_v = sc_out[0].rearrange("(k p) n -> p k n", p=P)
    down_v = ffn_down[0].rearrange("(f p) n -> p f n", p=P)
    ada_v = ada_w[0].rearrange("(k p) n -> k p n", p=P)

    with ExitStack() as ctx:
        arena_base = (nc.sbuf_base + 63) // 64 * 64
        arena_bytes = 204 * KIB
        ctx.enter_context(nc.sbuf_tensor("arena", [P, (arena_bytes + 64) // 4], F32))
        at = [arena_base]

        def region(size):
            start = at[0]
            at[0] += (size + 31) // 32 * 32
            assert at[0] <= arena_base + arena_bytes, "arena"
            return start

        def place(name, shape, dt, offset):
            return nc.alloc_sbuf_tensor_at(name, shape, dt, offset=offset)

        h_hi = place("h_hi", [P, NB, NK, BLOCK], F32R, region(32 * KIB))
        h_lo_at = region(32 * KIB)
        h_lo = place("h_lo", [P, NB, NK, BLOCK], F32R, h_lo_at)
        raw = place("raw", [P, 2, D], F32, region(8 * KIB))
        w_hi = place("w_hi", [P, 4, D], F32R, region(16 * KIB))
        w_lo = place("w_lo", [P, 4, D], F32R, region(16 * KIB))
        x1_at = region(32 * KIB)
        x1 = place("x1", [P, NT, D], F32, x1_at)
        Y_at = region(32 * KIB)
        y = place("y", [P, NK, SPAN], F32, Y_at)
        mid_hi = [place(f"mid_hi{p}", [P, 2, SPAN], F32R, Y_at + p * 16 * KIB) for p in range(2)]
        mid_lo = [place(f"mid_lo{p}", [P, 2, SPAN], F32R, Y_at + (16 * p + 8) * KIB) for p in range(2)]
        YS_at = region(16 * KIB)
        y_hi = place("y_hi", [P, 2, 2, BLOCK], F32R, YS_at)
        y_lo = place("y_lo", [P, 2, 2, BLOCK], F32R, YS_at + 8 * KIB)
        us = place("us", [P, 2, SPAN + 8], F32, YS_at)
        gated = place("gated", [P, 2, BLOCK], F32, YS_at + 2 * (SPAN + 8) * 4)
        m_at = x1_at + 32 * KIB - (SPAN + 8) * 4
        m = place("m", [P, SPAN + 8], F32, m_at)
        ada_sum = place("ada_sum", [P, 2 * D], F32, x1_at + 16 * KIB)
        stage_y = place("stage_y", [P, TB, D], F32, Y_at + 16 * KIB)
        stage_h = place("stage_h", [P, TB, D], F32, h_lo_at + 16 * KIB)
        ada_tile = [place(f"ada_tile{i}", [P, 2 * D], F32, start + (i % 2) * 8 * KIB)
                    for i, start in enumerate((YS_at, YS_at, x1_at, x1_at,
                                               Y_at, Y_at, arena_base + 16 * KIB, arena_base + 16 * KIB))]
        gate_row = place("gate_row", [P, 2, D], F32, region(8 * KIB))
        scratch_at = region(4 * KIB)
        c_copy = place("c_copy", [P, NB, BLOCK], F32, scratch_at)
        square_out = place("square_out", [P, D], BF16, scratch_at)
        tmp = place("tmp", [P, BLOCK], F32, scratch_at + 2 * KIB)
        ident = place("ident", [P, P], F32, region(512))
        ones = place("ones", [P, P], F32, region(512))
        vec_rows = place("vec_rows", [P, 2, P], F32, region(1024))

        V_ADA, V_C = 0, 6 * NK
        V_GM, V_GF = V_C + NK, V_C + 2 * NK
        V_SC = V_GF + NK
        ROWS0 = V_SC + TAPS * NK
        V_FC, ROWS1 = ROWS0, TAPS * NF
        cols = place("cols", [P, ROWS0 + ROWS1], F32, region(4 * (ROWS0 + ROWS1)))
        cond = place("cond", [P, NK], F32, region(32))
        scale_c = place("scale_c", [P, 2, NK], F32, region(64))
        shift_c = place("shift_c", [P, 2, NK], F32, region(64))
        mod_tmp = place("mod_tmp", [P, NK], F32, region(32))
        sumsq = place("sumsq", [P, 4 * NT], F32, region(128))
        mean_sq = place("mean_sq", [P, 4 * NT], F32, region(128))
        rstd = place("rstd", [P, 4 * NT], F32, region(128))
        minus_half = place("minus_half", [P, 1], F32, region(32))
        m_halo = place("m_halo", [P, NK, 2], F32, region(NK * 8))
        u_halo = place("u_halo", [P, NF, 2], F32, region(NF * 8))

        ps = ctx.enter_context(nc.psum_tensor("ps", [P, 8, BLOCK], F32))

        def sem(name):
            return ctx.enter_context(nc.semaphore(name))

        vec_loaded, gate_bias_loaded = sem("vec_loaded"), sem("gate_bias_loaded")
        const_made, ident_zeroed = sem("const_made"), sem("ident_zeroed")
        vec_transposed, cols_made, cond_made = sem("vec_transposed"), sem("cols_made"), sem("cond_made")
        early_ada_loaded = [sem(f"early_ada_loaded{i}") for i in range(8)]
        ada_loaded = [sem(f"ada_loaded{i}") for i in range(8)]
        ada_used, mod_reduced, mod_made = sem("ada_used"), sem("mod_reduced"), sem("mod_made")
        mod_step = sem("mod_step")
        raw_loaded = [sem(f"raw_loaded{i}") for i in range(2)]
        w_hi_made, w_ready, w_used, gate_folded = sem("w_hi_made"), sem("w_ready"), sem("w_used"), sem("gate_folded")
        load_turns, split_turns = sem("load_turns"), sem("split_turns")
        x_staged = [sem(f"x_staged{i}") for i in range(NT)]
        squared, rstd_made, rstd_step = sem("squared"), sem("rstd_made"), sem("rstd_step")
        normed, transposed = sem("normed"), sem("transposed")
        modulated, modulated_act = sem("modulated"), sem("modulated_act")
        h_hi_made = sem("h_hi_made")
        h_ready, h_ready_dve = sem("h_ready"), sem("h_ready_dve")
        early_transposed, early_hi_made, early_ready = sem("early_transposed"), sem("early_hi_made"), sem("early_ready")
        first_modulated = {"DVE": sem("first_modulated"), "ACT": sem("first_modulated_act")}
        proj_done, c_copied, m_made = sem("proj_done"), sem("c_copied"), sem("m_made")
        m_tapped, conv_step, y_made = sem("m_tapped"), sem("conv_step"), sem("y_made")
        y_hi_made, y_split, y_used = sem("y_hi_made"), sem("y_split"), sem("y_used")
        mixer_done, mixer_scaled, x1_made = sem("mixer_done"), sem("mixer_scaled"), sem("x1_made")
        x1_loaded = [sem(f"x1_loaded{i}") for i in range(NB)]
        up_done, u_tapped, ffn_conv_step = sem("up_done"), sem("u_tapped"), sem("ffn_conv_step")
        convolved, silu_made, gated_made = sem("convolved"), sem("silu_made"), sem("gated_made")
        mid_hi_made, mid_ready = sem("mid_hi_made"), sem("mid_ready")
        down_done, down_added, out_stored = sem("down_done"), sem("down_added"), sem("out_stored")

        VECTORS = [("shift", 0), ("scale", 0), ("gate", 0), ("shift", 1), ("scale", 1), ("gate", 1)]

        def ada_place(p, k):
            return (k, 1) if p == 0 else (k % 4, 2 * p + k // 4)

        def ada_count(p, k):
            return 2 * NK + NK * (p - 1) + k

        def half_of_pair(t, f):
            return t[:, f * D:(f + 1) * D].rearrange("p (v n) -> p v n", v=2)

        def tile_index(h, stage, t):
            return 2 * NT * h + NT * stage + t

        def stage_of(stage, t):
            return (stage_h if t < TB else stage_y)[:, t % TB, :]

        def by_halves(h, stage, t):
            return h == 0 and stage == 0 and t < TB

        def mod_count(h, stage, t):
            return tile_index(h, stage, t) + 1 - TB

        def first_mod_owner(t, f):
            return "DVE" if (t, f) == (0, 1) else "ACT"

        def first_mod_count(t, f):
            return sum(first_mod_owner(u % TB, u // TB) == first_mod_owner(t, f) for u in range(TB * f + t + 1))

        def lo_shares(h, stage, t, early=False):
            if by_halves(h, stage, t):
                return (slice(0, 4), None) if early else (slice(4, 6), slice(6, 8))
            n = 4 if t == NT - 1 else 6
            return slice(0, n), slice(n, NK)

        def bank_of(h, stage, t, k):
            if by_halves(h, stage, t):
                return (t if k < 4 else (1, 2, 3, 5)[t])
            if h == 0 and stage == 0:
                return ((2, 3), (1, 5))[t % 2][k // 4]
            return (4 if stage == 1 and t >= TB else 0) + 2 * (t % 2) + k // 4

        def proj_count(h, chunk, j, b, first=False):
            return 2 * 3 * NK * h + 2 * 3 * chunk + (3 * b + j if first else 2 * j + b) + 1

        def sum_bank(v):
            return 7 if v < 2 else 2

        ITEMS = NF * NB
        DOWNS = 2 * NT
        STORES = NT + 1
        NEXT_A = (0, 1, 2, 3, 5, 6, 7)
        block = ctx.enter_context(nc.Block())

        @block.sync
        def _(sp):
            def rows(dst, src):
                sp.dma_start(dst, src.rearrange("(r n) -> r n", n=P)).then_inc(vec_loaded, 16)

            def load_first_ada(f, ks):
                for k in ks:
                    src = ada_v[k][:, 0:2 * D].rearrange("p (v n) -> p v n", v=2)
                    sp.dma_start(half_of_pair(ada_tile[k], f),
                                 src[:, :, f * BLOCK:(f + 1) * BLOCK]
                                 ).then_inc((early_ada_loaded, ada_loaded)[f][k], 16)

            def load_ada(p, ks):
                for k in ks:
                    i, _ = ada_place(p, k)
                    sp.wait_ge(ada_used, ada_count(p, k) - 4 + 1)
                    sp.dma_start(ada_tile[i][:], ada_v[k][:, 2 * p * D:2 * (p + 1) * D]).then_inc(ada_loaded[i], 16)

            def load_raw(r, src, n):
                if not (isinstance(n, int) and n < 2):
                    sp.wait_ge(w_ready, n - 1)
                    sp.sem_inc(load_turns, 1)
                sp.dma_start(raw[:, r, :] if len(src.shape) == 2 else
                             raw[:, r, :].rearrange("p (a b) -> p a b", a=src.shape[1]),
                             src).then_inc(raw_loaded[r], 16)

            def sc_in_stripe(chunk, j):
                return sc_in_v[:, :, bass.ds(((j + 1) % 3) * D + chunk * P, P)]

            def up_stripe(chunk, j):
                return up_v[:, :, bass.ds(j * F + chunk * P, P)]

            def load_x(h, t):
                if h > 0 and t == 0:
                    sp.wait_ge(up_done, 2 * ITEMS * h)
                if h > 0 and t == TB:
                    sp.wait_ge(down_done, DOWNS * (GROUPS * h - 1))
                sp.dma_start(stage_of(0, t), x_t[NT * h + t]).then_inc(x_staged[t], 16)

            def load_b(U, pair):
                for j in range(6):
                    load_raw(j % 2, sc_in_stripe(2 * pair + j // 3, j % 3), U + 6 * pair + j)

            def load_residual(h, b):
                sp.dma_start(x1[:, TB * b:TB * b + TB, :],
                             x_t[NT * h + TB * b:NT * h + TB * b + TB].rearrange("t p d -> p t d")
                             ).then_inc(x1_loaded[b], 16)

            for h in range(HALVES):
                U = UNITS * h
                if h == 0:
                    load_first_ada(0, [0])
                    rows(vec_rows[V_C:V_GM, 0, :], c[0])
                    rows(vec_rows[V_ADA:V_C, 0, :], ada_b[0])
                    rows(vec_rows[V_GM:V_GF, 0, :], ln_mix_g[0])
                    load_first_ada(0, [1])
                    rows(vec_rows[V_GF:V_SC, 0, :], ln_ffn_g[0])
                    rows(vec_rows[V_SC:ROWS0, 0, :], sc_conv[0].rearrange("a n -> (a n)"))
                    rows(vec_rows[0:ROWS1, 1, :], ffn_conv[0].rearrange("a n -> (a n)"))
                    for t in range(TB):
                        load_first_ada(0, range(max(2 * t + 1, 2), min(2 * t + 3, NK)))
                        load_x(h, t)
                    load_raw(0, sc_in_stripe(0, 0), 0)
                    load_raw(1, sc_in_stripe(0, 1), 1)
                    load_first_ada(1, range(0, 6))
                    load_raw(0, sc_in_stripe(0, 2), 2)
                    load_first_ada(1, range(6, NK))
                    for t in range(TB, NT):
                        load_x(h, t)
                    for i, v in enumerate((2, 5)):
                        sp.dma_start(gate_row[:, i, :], ada_b[:, v * D:(v + 1) * D].broadcast_to([P, D])
                                     ).then_inc(gate_bias_loaded, 16)
                    load_ada(1, range(4))
                    load_raw(1, sc_in_stripe(1, 0), 3)
                    load_raw(0, sc_in_stripe(1, 1), 4)
                    load_ada(1, range(4, 8))
                    load_raw(1, sc_in_stripe(1, 2), 5)
                    for j in range(6, 9):
                        load_raw(j % 2, sc_in_stripe(j // 3, j % 3), j)
                    load_ada(2, range(4))
                    for j in range(9, 12):
                        load_raw(j % 2, sc_in_stripe(j // 3, j % 3), j)
                    load_ada(2, range(4, 8))
                else:
                    for j in range(4, 6):
                        load_raw(j % 2, sc_in_stripe(j // 3, j % 3), U + j)
                with sp.Fori(2 if h == 0 else 1, NK // 2) as pair:
                    load_b(U, pair)
                if h == 0:
                    sp.wait_ge(mod_made, len(VECTORS))
                else:
                    sp.wait_ge(out_stored, 16 * STORES * h)
                load_residual(h, 0)
                for i in range(UC):
                    dh, s = divmod(i, NK // 2)
                    load_raw(i % 2, sc_out_v[:, 2 * s:2 * s + 2, dh * BLOCK:(dh + 1) * BLOCK], U + C0 + i)
                    if i == 4:
                        sp.wait_ge(y_made, NK * NB * (h + 1))
                        load_residual(h, 1)
                for i in range(UP):
                    load_raw(i % 2, up_stripe(i // 2, i % 2), U + P0 + i)
                with sp.Fori(0, (GROUPS - 1) // 2) as g2:
                    for e in range(2):
                        for i in range(4):
                            load_raw(i % 2, up_stripe(4 * g2 + 2 * e + 2 + i // 2, i % 2),
                                     U + E0 + 12 * g2 + 6 * e + i)
                        for i in range(2):
                            load_raw(i % 2, down_v[:, bass.ds(4 * g2 + 2 * e + i, 1), :],
                                     U + E0 + 12 * g2 + 6 * e + 4 + i)
                for i in range(2):
                    load_raw(i % 2, down_v[:, 2 * (GROUPS - 1) + i, :], U + L0 + i)
                if h + 1 < HALVES:
                    for t in range(TB):
                        load_x(h + 1, t)
                    load_raw(0, sc_in_stripe(0, 0), U + UNITS)
                    load_raw(1, sc_in_stripe(0, 1), U + UNITS + 1)
                    for t in range(TB, NT):
                        load_x(h + 1, t)
                    for j in range(2, 4):
                        load_raw(j % 2, sc_in_stripe(j // 3, j % 3), U + UNITS + j)
                for t in range(NT - 1):
                    sp.wait_ge(down_added, DOWNS * (GROUPS * (h + 1) - 1) + 2 * t + 2 + 4)
                    sp.dma_start(out_t[NT * h + t], x1[:, t, :]).then_inc(out_stored, 16)
                for dh in range(2):
                    cut = slice(dh * BLOCK, (dh + 1) * BLOCK)
                    sp.wait_ge(down_added, DOWNS * (GROUPS * (h + 1) - 1) + DOWNS - 1 + dh + 4)
                    sp.dma_start(out_t[NT * h + NT - 1][:, cut], x1[:, NT - 1, cut]).then_inc(out_stored, 16)
            sp.wait_ge(out_stored, 16 * STORES * HALVES)

        @block.gpsimd
        def _(pool):
            pool.memset(ident[:], 0.0).then_inc(ident_zeroed, 1)
            pool.memset(ones[:], 1.0)
            pool.memset(minus_half[:], -0.5)
            pool.memset(m_halo[:], 0.0)
            pool.memset(u_halo[:], 0.0)
            pool.wait_ge(ident_zeroed, 1)
            pool.affine_select(out=ident[:], in_=ident[:], compare_op=ALU.not_equal, fill=1.0,
                               base=0, pattern=[[-1, P]], channel_multiplier=1).then_inc(const_made, 1)
            def split(n, n2, slot, used, gate=None):
                r, m = n2
                pool.wait_ge(raw_loaded[r], 16 * (m + 1))
                if used is not None:
                    pool.wait_ge(w_used, used)
                if gate is not None:
                    pool.tensor_tensor(raw[:, r, :], raw[:, r, :], gate_row[:, 1, :], ALU.mult).then_inc(gate_folded, 1)
                    pool.wait_ge(gate_folded, gate)
                pool.sem_inc(split_turns, 1)
                pool.tensor_scalar(w_hi[:, slot, :], raw[:, r, :], 1.0, 1.0, ALU.mult, ALU.mult).then_inc(w_hi_made, 1)
                pool.wait_ge(w_hi_made, n + 1)
                pool.tensor_tensor(w_lo[:, slot, :], raw[:, r, :], w_hi[:, slot, :].bitcast(F32),
                                   ALU.subtract).then_inc(w_ready, 1)

            def take_rstd(h, stage, t):
                i = tile_index(h, stage, t)
                pool.wait_ge(squared, i + 1)
                pool.tensor_scalar(mean_sq[:, i:i + 1], sumsq[:, i:i + 1], 1.0 / D, RMS_EPS,
                                   ALU.mult, ALU.add).then_inc(rstd_step, 1)
                pool.wait_ge(rstd_step, i + 1)
                pool.tensor_tensor(rstd[:, i:i + 1], mean_sq[:, i:i + 1], minus_half[:], ALU.pow).then_inc(rstd_made, 1)

            def norm(t):
                pool.wait_ge(rstd_made, t + 1)
                pool.tensor_scalar(stage_of(0, t), stage_of(0, t), rstd[:, t:t + 1], 1.0, ALU.mult, ALU.mult
                                   ).then_inc(normed, 1)

            def make_h_lo(h, stage, t, early=False):
                i = tile_index(h, stage, t)
                b, tt = divmod(t, TB)
                cut = slice(tt * P, tt * P + P)
                ks = lo_shares(h, stage, t, early)[0]
                pool.wait_ge(early_hi_made if early else h_hi_made, i + 1)
                if t >= TB:
                    pool.wait_ge(h_ready, i)
                    pool.wait_ge(h_ready_dve, tile_index(h, stage, TB))
                pool.tensor_tensor(h_lo[:, b, ks, cut], stage_of(stage, t).rearrange("p (k n) -> p k n", k=NK)[:, ks],
                                   h_hi[:, b, ks, cut].bitcast(F32), ALU.subtract
                                   ).then_inc(early_ready if early else h_ready, 1)

            def split_at(U, i, extra=0, extra_raw=0, gate=None):
                o = occupant_of(i)
                used = None if U + o < 0 else U + o + 1 + extra
                split(U + i + extra, (i % 2, (U + i) // 2 + extra_raw), slot_of(i), used, gate)

            for h in range(HALVES):
                U = UNITS * h
                for t in range(TB):
                    take_rstd(h, 0, t)
                split_at(U, 0)
                split_at(U, 1)
                if h == 0:
                    for t in range(TB):
                        make_h_lo(h, 0, t, early=True)
                    split_at(U, 2)
                    for t in range(TB, TB + 2):
                        take_rstd(h, 0, t)
                        norm(t)
                    for t in range(TB):
                        make_h_lo(h, 0, t)
                    for t in range(TB + 2, NT):
                        take_rstd(h, 0, t)
                        norm(t)
                else:
                    for t in range(TB):
                        make_h_lo(h, 0, t)
                        take_rstd(h, 0, TB + t)
                for t in range(TB, NT - 1):
                    make_h_lo(h, 0, t)
                if h > 0:
                    split_at(U, 2)
                make_h_lo(h, 0, NT - 1)
                for i in range(3, 6):
                    split_at(U, i)
                with pool.Fori(0, NK // 2 - 1) as pair:
                    for i in range(6, 12):
                        split_at(U, i, 6 * pair, 3 * pair)
                for i in range(C0, P0):
                    split_at(U, i)
                take_rstd(h, 1, 0)
                take_rstd(h, 1, 1)
                split_at(U, P0)
                take_rstd(h, 1, 2)
                take_rstd(h, 1, 3)
                make_h_lo(h, 1, 0)
                split_at(U, P0 + 1)
                for t in range(1, TB):
                    make_h_lo(h, 1, t)
                take_rstd(h, 1, TB)
                take_rstd(h, 1, TB + 1)
                split_at(U, P0 + 2)
                take_rstd(h, 1, TB + 2)
                take_rstd(h, 1, TB + 3)
                make_h_lo(h, 1, TB)
                split_at(U, P0 + 3)
                for t in range(TB + 1, NT):
                    make_h_lo(h, 1, t)
                if h == 0:
                    pool.wait_ge(mod_made, len(VECTORS))
                folded = 2 * GROUPS * h
                with pool.Fori(0, (GROUPS - 1) // 2) as g2:
                    for j in range(12):
                        e, i = divmod(j, 6)
                        split_at(U, E0 + j, 12 * g2, 6 * g2,
                                 gate=folded + 4 * g2 + 2 * e + i - 4 + 1 if i >= 4 else None)
                for i in range(2):
                    split_at(U, L0 + i, gate=folded + 2 * (GROUPS - 1) + i + 1)

        @block.scalar
        def _(act):
            def square(h, stage, t):
                i = tile_index(h, stage, t)
                if stage == 0:
                    act.wait_ge(x_staged[t], 16 * (h + 1))
                    src = stage_of(stage, t)
                else:
                    act.wait_ge(x1_made, 2 * NT * h + NT + t + 1)
                    src = x1[:, t, :]
                if i > 0:
                    act.wait_ge(squared, i)
                act.activation(square_out[:], src, ACT.Square, accum_out=sumsq[:, i:i + 1]).then_inc(squared, 1)

            def norm(h, stage, t):
                i = tile_index(h, stage, t)
                act.wait_ge(rstd_made, i + 1)
                src = stage_of(stage, t) if stage == 0 else x1[:, t, :]
                act.activation(stage_of(stage, t), src, ACT.Copy, scale=rstd[:, i:i + 1]).then_inc(normed, 1)

            def modulate(h, stage, t, early=False):
                i = tile_index(h, stage, t)
                ks = range(NK // 2, NK)
                done = modulated_act
                if by_halves(h, stage, t):
                    ks = range(NK // 2) if early else range(NK // 2, NK)
                    done = first_modulated["ACT"]
                dst = stage_of(stage, t)
                act.wait_ge(early_transposed if early else transposed, i + 1)
                for k in ks:
                    op = act.activation(dst[:, k * P:(k + 1) * P], ps[:, bank_of(h, stage, t, k), (k % 4) * P:(k % 4 + 1) * P],
                                        ACT.Identity, scale=scale_c[:, stage, k:k + 1], bias=shift_c[:, stage, k:k + 1])
                op.then_inc(done, 1)

            def stage_b(h, chunk, first=False):
                N = NB * NK * h
                for b in range(NB):
                    act.wait_ge(proj_done, proj_count(h, chunk, 0, b, first))
                    act.activation(c_copy[:, b, :], ps[:, 4 + b, :], ACT.Copy).then_inc(c_copied, 1)
                for b in range(NB):
                    act.wait_ge(m_made, N + NB * chunk + b + 1)
                    act.activation(y[:, bass.ds(chunk, 1), b * BLOCK:(b + 1) * BLOCK],
                                   m[:, 2 + b * BLOCK:2 + (b + 1) * BLOCK].unsqueeze(1), ACT.Copy,
                                   scale=cols[:, bass.ds(V_SC + 2 * NK + chunk, 1)]).then_inc(m_tapped, 1)

            def make_y_hi(h, n):
                dh, grp, s = n // 8, n // 4 % 2, n % 4
                if n < 2:
                    act.wait_ge(y_made, NB * (NK * h + NK - 1))
                elif n == 3:
                    act.wait_ge(y_made, NB * NK * (h + 1) - 1)
                elif n == 4:
                    act.wait_ge(y_made, NB * NK * (h + 1))
                if n >= 2:
                    act.wait_ge(y_used, 15 * h + n - 1)
                act.activation(y_hi[:, n % 2], y[:, 2 * s:2 * s + 2, grp * BLOCK:(grp + 1) * BLOCK],
                               ACT.Copy).then_inc(y_hi_made, 1)

            def ffn_item(h, q, qe, chunk, chunk_e, b, par, j):
                Q = ITEMS * h + q + qe
                pp = q % 2
                u_bank, ce = 2 * pp, chunk + chunk_e
                act.wait_ge(up_done, 2 * Q + 1)
                if b == 0:
                    act.activation(us[:, j, 0:2], u_halo[:, bass.ds(ce, 1), :].rearrange("p a b -> p (a b)"), ACT.Copy)
                act.activation(us[:, j, 2 + b * BLOCK:2 + (b + 1) * BLOCK], ps[:, u_bank, :], ACT.Copy)
                if b == NB - 1 and h + 1 < HALVES:
                    act.activation(u_halo[:, bass.ds(ce, 1), :].rearrange("p a b -> p (a b)"),
                                   ps[:, u_bank, BLOCK - 2:BLOCK], ACT.Copy)
                act.activation(gated[:, pp, :], ps[:, u_bank, :], ACT.Copy,
                               scale=cols[:, bass.ds(V_FC + 2 * NF + ce, 1)]).then_inc(u_tapped, 1)
                act.wait_ge(convolved, Q + 1)
                act.activation(gated[:, pp, :], gated[:, pp, :], ACT.Silu).then_inc(silu_made, 1)
                act.wait_ge(gated_made, Q + 1)
                act.activation(mid_hi[par][:, j, b * BLOCK:(b + 1) * BLOCK], gated[:, pp, :], ACT.Copy).then_inc(mid_hi_made, 1)

            act.wait_ge(const_made, 1)
            act.wait_ge(cols_made, 1)
            act.activation(cond[:], cols[:, V_C:V_GM], ACT.Silu).then_inc(cond_made, 1)

            def norm_block(h, stage, t0):
                square(h, stage, t0)
                for t in range(t0 + 1, t0 + TB):
                    square(h, stage, t)
                    norm(h, stage, t - 1)
                norm(h, stage, t0 + TB - 1)

            norm_block(0, 0, 0)
            act.wait_ge(mod_made, 1)
            for t in range(TB):
                modulate(0, 0, t, early=True)
            for t in range(TB, TB + 3):
                square(0, 0, t)
            act.wait_ge(mod_made, 2)
            for t in range(1, TB):
                modulate(0, 0, t)
            square(0, 0, TB + 3)
            for t in range(TB, NT):
                modulate(0, 0, t)
            for h in range(HALVES):
                stage_b(h, 0, first=True)
                with act.Fori(1, NK) as chunk:
                    stage_b(h, chunk)
                for n in range(14):
                    make_y_hi(h, n)
                square(h, 1, 0)
                square(h, 1, 1)
                norm(h, 1, 0)
                make_y_hi(h, 14)
                norm(h, 1, 1)
                square(h, 1, 2)
                square(h, 1, 3)
                modulate(h, 1, 0)
                make_y_hi(h, 15)
                norm(h, 1, 2)
                modulate(h, 1, 1)
                norm(h, 1, 3)
                modulate(h, 1, 2)
                modulate(h, 1, 3)
                square(h, 1, TB)
                for t in range(TB + 1, NT):
                    square(h, 1, t)
                    if t < NT - 1:
                        norm(h, 1, t - 1)
                modulate(h, 1, TB)
                norm(h, 1, NT - 2)
                norm(h, 1, NT - 1)
                modulate(h, 1, TB + 1)
                modulate(h, 1, TB + 2)
                modulate(h, 1, TB + 3)
                ffn_item(h, 0, 0, 0, 0, 0, 0, 0)
                ffn_item(h, 1, 0, 1, 0, 0, 0, 1)
                ffn_item(h, 2, 0, 0, 0, 1, 0, 0)
                ffn_item(h, 3, 0, 1, 0, 1, 0, 1)
                with act.Fori(0, (GROUPS - 1) // 2) as g2:
                    for e in range(2):
                        for i in range(4):
                            ffn_item(h, 4 + 4 * e + i, 8 * g2, 2 + 2 * e + i // 2, 4 * g2, i % 2, 1 - e, i // 2)

                if h + 1 < HALVES:
                    norm_block(h + 1, 0, 0)
                    modulate(h + 1, 0, 0)
                    square(h + 1, 0, TB)
                    for t in range(1, TB):
                        modulate(h + 1, 0, t)
                        norm(h + 1, 0, TB + t - 1)
                        square(h + 1, 0, TB + t)
                    norm(h + 1, 0, NT - 1)
                    for t in range(TB, NT):
                        modulate(h + 1, 0, t)

        @block.vector
        def _(dve):
            def add_product(ada_sum, tile, k, n):
                if k == 0:
                    dve.tensor_scalar(ada_sum, tile, cond[:, k:k + 1], None, ALU.mult).then_inc(ada_used, 1)
                else:
                    dve.wait_ge(ada_used, n)
                    dve.scalar_tensor_tensor(out=ada_sum, in0=tile, scalar=cond[:, k:k + 1], in1=ada_sum,
                                             op0=ALU.mult, op1=ALU.add).then_inc(ada_used, 1)

            def first_ada_products(f, ks):
                for k in ks:
                    dve.wait_ge((early_ada_loaded, ada_loaded)[f][k], 16)
                    add_product(ada_sum[:, f * D:(f + 1) * D], ada_tile[k][:, f * D:(f + 1) * D], k, NK * f + k)

            def ada_products(p, ks):
                for k in ks:
                    i, m = ada_place(p, k)
                    dve.wait_ge(ada_loaded[i], 16 * m)
                    if k == 0:
                        dve.wait_ge(mod_reduced, 2 * p)
                    add_product(ada_sum[:], ada_tile[i][:], k, ada_count(p, k))

            def first_mod_vectors(f):
                ks = slice(f * NK // 2, (f + 1) * NK // 2)
                shift, scale = (ps[:, sum_bank(0), (2 * f + v) * 4:(2 * f + v + 1) * 4] for v in range(2))
                dve.wait_ge(mod_reduced, f + 1)
                dve.tensor_tensor(shift_c[:, 0, ks], shift, cols[:, V_ADA:V_ADA + NK][:, ks], ALU.add)
                dve.tensor_tensor(mod_tmp[:, ks], scale, cols[:, V_ADA + NK:V_ADA + 2 * NK][:, ks], ALU.add).then_inc(mod_step, 1)
                dve.wait_ge(mod_step, f + 1)
                dve.scalar_tensor_tensor(out=scale_c[:, 0, ks], in0=mod_tmp[:, ks], scalar=1.0,
                                         in1=cols[:, V_GM:V_GF][:, ks], op0=ALU.add, op1=ALU.mult).then_inc(mod_made, 1)

            def mod_vector(v):
                kind, which = VECTORS[v]
                bias = cols[:, V_ADA + v * NK:V_ADA + (v + 1) * NK]
                dve.wait_ge(mod_reduced, v + 1)
                if kind == "gate":
                    dve.wait_ge(gate_bias_loaded, 32)
                    dve.tensor_tensor(gate_row[:, which, 0:BLOCK], ps[:, sum_bank(v), :], gate_row[:, which, 0:BLOCK], ALU.add)
                    dve.tensor_tensor(gate_row[:, which, BLOCK:D], ps[:, sum_bank(v) + 1, :], gate_row[:, which, BLOCK:D],
                                      ALU.add).then_inc(mod_made, 1)
                elif kind == "shift":
                    dve.tensor_tensor(shift_c[:, which, :], ps[:, sum_bank(v), 0:NK], bias, ALU.add).then_inc(mod_made, 1)
                else:
                    dve.tensor_tensor(mod_tmp[:], ps[:, sum_bank(v), 0:NK], bias, ALU.add).then_inc(mod_step, 1)
                    dve.wait_ge(mod_step, 3)
                    dve.scalar_tensor_tensor(out=scale_c[:, which, :], in0=mod_tmp[:], scalar=1.0,
                                             in1=cols[:, V_GF:V_SC], op0=ALU.add, op1=ALU.mult).then_inc(mod_made, 1)

            def modulate(h, stage, t, early=False):
                i = tile_index(h, stage, t)
                ks, made = range(NK // 2), range(NK)
                halves = by_halves(h, stage, t)
                if halves:
                    made = range(NK // 2) if early else range(NK // 2, NK)
                    ks = made if first_mod_owner(t, made[0] // 4) == "DVE" else ()
                dst = stage_of(stage, t)
                if len(ks):
                    dve.wait_ge(early_transposed if early else transposed, i + 1)
                for k in ks:
                    op = dve.tensor_scalar(dst[:, k * P:(k + 1) * P],
                                           ps[:, bank_of(h, stage, t, k), (k % 4) * P:(k % 4 + 1) * P],
                                           scale_c[:, stage, k:k + 1], shift_c[:, stage, k:k + 1], ALU.mult, ALU.add)
                if len(ks):
                    op.then_inc(first_modulated["DVE"] if halves else modulated, 1)
                b, tt = divmod(t, TB)
                if halves:
                    f = 0 if early else 1
                    dve.wait_ge(first_modulated[first_mod_owner(t, f)], first_mod_count(t, f))
                else:
                    dve.wait_ge(modulated, mod_count(h, stage, t))
                    dve.wait_ge(modulated_act, mod_count(h, stage, t))
                made = slice(made[0], made[-1] + 1)
                dve.tensor_copy(h_hi[:, b, made, tt * P:tt * P + P],
                                dst.rearrange("p (k n) -> p k n", k=NK)[:, made]
                                ).then_inc(early_hi_made if early else h_hi_made, 1)
                lo = lo_shares(h, stage, t, early)[1]
                if lo is not None:
                    dve.wait_ge(h_hi_made, i + 1)
                    if t == TB:
                        dve.wait_ge(h_ready, i)
                        dve.wait_ge(h_ready_dve, i)
                    dve.tensor_tensor(h_lo[:, b, lo, tt * P:tt * P + P], dst.rearrange("p (k n) -> p k n", k=NK)[:, lo],
                                      h_hi[:, b, lo, tt * P:tt * P + P].bitcast(F32), ALU.subtract).then_inc(h_ready_dve, 1)

            def stage_b(h, chunk, first=False, last=False):
                N = NB * NK * h

                def tap(w):
                    return cols[:, bass.ds(V_SC + w * NK + chunk, 1)]

                def yb(b):
                    return y[:, bass.ds(chunk, 1), b * BLOCK:(b + 1) * BLOCK].rearrange("p a n -> p (a n)")

                halo = m_halo[:, bass.ds(chunk, 1), :].rearrange("p a n -> p (a n)")
                dve.tensor_copy(m[:, 0:2], halo)
                for b in range(NB):
                    dve.wait_ge(c_copied, N + NB * chunk + b + 1)
                    dve.wait_ge(proj_done, proj_count(h, chunk, 1, b, first))
                    dve.tensor_tensor(m[:, 2 + b * BLOCK:2 + (b + 1) * BLOCK], ps[:, 6 + b, :], c_copy[:, b, :],
                                      ALU.mult).then_inc(m_made, 1)
                for b in range(NB):
                    dve.wait_ge(m_tapped, N + NB * chunk + b + 1)
                    dve.scalar_tensor_tensor(out=yb(b), in0=m[:, 1 + b * BLOCK:1 + (b + 1) * BLOCK], scalar=tap(1),
                                             in1=yb(b), op0=ALU.mult, op1=ALU.add).then_inc(conv_step, 1)
                if h + 1 < HALVES:
                    dve.tensor_copy(halo, m[:, SPAN:SPAN + 2])
                for b in range(NB):
                    dve.wait_ge(conv_step, 2 * N + 2 * NB * chunk + b + 1)
                    dve.scalar_tensor_tensor(out=yb(b), in0=m[:, b * BLOCK:(b + 1) * BLOCK], scalar=tap(0),
                                             in1=yb(b), op0=ALU.mult, op1=ALU.add).then_inc(conv_step, 1)
                if last:
                    make_y_lo(h, 0)
                    make_y_lo(h, 1)
                for b in range(NB):
                    dve.wait_ge(conv_step, 2 * N + 2 * NB * chunk + NB + b + 1)
                    dve.wait_ge(proj_done, proj_count(h, chunk, 2, b, first))
                    dve.tensor_tensor(yb(b), ps[:, b, :], yb(b), ALU.mult).then_inc(y_made, 1)

            def make_y_lo(h, n):
                grp, s = n // 4 % 2, n % 4
                dve.wait_ge(y_hi_made, 16 * h + n + 1)
                dve.tensor_tensor(y_lo[:, n % 2], y[:, 2 * s:2 * s + 2, grp * BLOCK:(grp + 1) * BLOCK],
                                  y_hi[:, n % 2].bitcast(F32), ALU.subtract).then_inc(y_split, 1)

            def residual(h, group):
                dh, grp = divmod(group, 2)
                cut = slice(dh * BLOCK, (dh + 1) * BLOCK)
                if h == 0 and group == 0:
                    dve.wait_ge(mod_made, len(VECTORS))
                if dh == 0:
                    dve.wait_ge(x1_loaded[grp], 16 * (h + 1))
                for i in range(TB):
                    n = 16 * h + 4 * group + i
                    t = TB * grp + i
                    dve.wait_ge(mixer_done, n + 1)
                    if n > 0:
                        dve.wait_ge(x1_made, n)
                    dve.tensor_tensor(tmp[:], ps[:, 4 + i, :], gate_row[:, 0, cut], ALU.mult).then_inc(mixer_scaled, 1)
                    dve.wait_ge(mixer_scaled, n + 1)
                    dve.tensor_tensor(x1[:, t, cut], tmp[:], x1[:, t, cut], ALU.add).then_inc(x1_made, 1)

            def ffn_item(h, q, qe, chunk, chunk_e, b, par, j):
                Q = ITEMS * h + q + qe
                pp = q % 2
                ce = chunk + chunk_e
                g = gated[:, pp, :]

                def tap(w):
                    return cols[:, bass.ds(V_FC + w * NF + ce, 1)]

                dve.wait_ge(u_tapped, Q + 1)
                dve.scalar_tensor_tensor(out=g, in0=us[:, j, 1 + b * BLOCK:1 + (b + 1) * BLOCK], scalar=tap(1),
                                         in1=g, op0=ALU.mult, op1=ALU.add).then_inc(ffn_conv_step, 1)
                dve.wait_ge(ffn_conv_step, Q + 1)
                dve.scalar_tensor_tensor(out=g, in0=us[:, j, b * BLOCK:(b + 1) * BLOCK], scalar=tap(0),
                                         in1=g, op0=ALU.mult, op1=ALU.add).then_inc(convolved, 1)
                dve.wait_ge(silu_made, Q + 1)
                dve.wait_ge(up_done, 2 * Q + 2)
                dve.tensor_tensor(g, ps[:, 2 * pp + 1, :], g, ALU.mult).then_inc(gated_made, 1)
                dve.wait_ge(mid_hi_made, Q + 1)
                cut = slice(b * BLOCK, (b + 1) * BLOCK)
                dve.tensor_tensor(mid_lo[par][:, j, cut], g, mid_hi[par][:, j, cut].bitcast(F32),
                                  ALU.subtract).then_inc(mid_ready, 1)

            def add_down(h, g, ge, next_a=False):
                N = DOWNS * (GROUPS * h + g + ge)
                for r in range(DOWNS):
                    t, dh = divmod(r, 2)
                    cut = slice(dh * BLOCK, (dh + 1) * BLOCK)
                    dve.wait_ge(down_done, N + r + 1)
                    dve.tensor_tensor(x1[:, t, cut], ps[:, 4 + r % 4, :], x1[:, t, cut], ALU.add).then_inc(down_added, 1)
                    if next_a and dh == 1 and t in NEXT_A:
                        modulate(h + 1, 0, NEXT_A.index(t))

            dve.sem_inc(down_added, 4)
            dve.wait_ge(const_made, 1)
            dve.wait_ge(vec_transposed, 1)
            dve.tensor_copy(cols[:], ps[:, 2, 0:ROWS0 + ROWS1]).then_inc(cols_made, 1)
            dve.wait_ge(cond_made, 1)
            first_ada_products(0, range(NK))
            first_ada_products(1, range(1))
            first_mod_vectors(0)
            for t in range(TB):
                if t != 2:
                    first_ada_products(1, [1 + t - t // 3])
                modulate(0, 0, t, early=True)
            first_ada_products(1, range(TB, NK))
            first_mod_vectors(1)
            dve.wait_ge(mod_made, 2)
            for t in range(NT):
                modulate(0, 0, t)
            for h in range(HALVES):
                if h == 0:
                    for chunk in range(4):
                        ada_products(1 + chunk // 2, range(4 * (chunk % 2), 4 * (chunk % 2) + 4))
                        stage_b(h, chunk, first=chunk == 0)
                        if chunk % 2 == 1:
                            mod_vector(chunk + 1)
                            mod_vector(chunk + 2)
                else:
                    dve.wait_ge(out_stored, 16 * STORES * h)
                    stage_b(h, 0, first=True)
                with dve.Fori(4 if h == 0 else 1, NK - 1) as chunk:
                    stage_b(h, chunk)
                stage_b(h, NK - 1, last=True)
                for n in range(2, 15):
                    make_y_lo(h, n)
                    if n % 4 == 0:
                        residual(h, n // 4 - 1)
                modulate(h, 1, 0)
                make_y_lo(h, 15)
                for t in range(1, TB):
                    modulate(h, 1, t)
                residual(h, 3)
                modulate(h, 1, TB)
                modulate(h, 1, TB + 1)
                modulate(h, 1, TB + 2)
                modulate(h, 1, TB + 3)
                ffn_item(h, 0, 0, 0, 0, 0, 0, 0)
                ffn_item(h, 1, 0, 1, 0, 0, 0, 1)
                ffn_item(h, 2, 0, 0, 0, 1, 0, 0)
                ffn_item(h, 3, 0, 1, 0, 1, 0, 1)
                with dve.Fori(0, (GROUPS - 1) // 2) as g2:
                    for e in range(2):
                        for i in range(4):
                            ffn_item(h, 4 + 4 * e + i, 8 * g2, 2 + 2 * e + i // 2, 4 * g2, i % 2, 1 - e, i // 2)
                        add_down(h, e, 2 * g2)
                add_down(h, GROUPS - 1, 0, h + 1 < HALVES)
                if h + 1 < HALVES:
                    for t in range(len(NEXT_A), NT):
                        modulate(h + 1, 0, t)

        @block.tensor
        def _(pe):
            def products(bank, pairs, start=True, stop=True, gone=(), first_done=None):
                last = len(pairs) - 1
                gone = list(gone)
                for i, ((s_hi, s_lo), (v_hi, v_lo)) in enumerate(pairs):
                    a = pe.matmul(ps[:, bank, :], s_hi, v_hi, start=start and i == 0, stop=False)
                    b = pe.matmul(ps[:, bank, :], s_hi, v_lo, start=False, stop=False)
                    op = pe.matmul(ps[:, bank, :], s_lo, v_hi, start=False, stop=stop and i == last)
                    if i == 0:
                        for done, signal in zip((a, b), gone):
                            done.then_inc(signal, 1)
                        if first_done is not None:
                            op.then_inc(first_done, 1)
                return op

            def project(slot, b, bank, gone=(), ks=range(NK)):
                return products(bank, [((w_hi[:, slot, k * P:(k + 1) * P], w_lo[:, slot, k * P:(k + 1) * P]),
                                        (h_hi[:, b, k, :], h_lo[:, b, k, :])) for k in ks],
                                ks[0] == 0, ks[-1] == NK - 1, gone=gone)

            def transpose_tile(h, stage, t, early=False):
                i = tile_index(h, stage, t)
                src = stage_of(stage, t)
                pe.wait_ge(normed, i + 1)
                ks = range(NK)
                if by_halves(h, stage, t):
                    ks = range(NK // 2) if early else range(NK // 2, NK)
                    if not early:
                        pe.wait_ge(first_modulated["ACT"], first_mod_count(min(t + 1, TB - 1), 0))
                if stage == 1 and t == TB:
                    pe.wait_ge(x1_made, 16 * h + 16)
                before = [u for u in range(t) if bank_of(h, stage, u, NK - 1) == bank_of(h, stage, t, NK - 1)]
                if h == 0 and stage == 0 and t == TB:
                    pe.wait_ge(first_modulated["ACT"], first_mod_count(2, 1))
                elif h == 0 and stage == 0 and t == TB + 1:
                    pe.wait_ge(first_modulated["DVE"], first_mod_count(0, 1))
                    pe.wait_ge(first_modulated["ACT"], first_mod_count(TB - 1, 1))
                elif before:
                    pe.wait_ge(modulated, mod_count(h, stage, before[-1]))
                    pe.wait_ge(modulated_act, mod_count(h, stage, before[-1]))
                for k in ks:
                    op = pe.transpose(ps[:, bank_of(h, stage, t, k), (k % 4) * P:(k % 4 + 1) * P],
                                      src[:, k * P:(k + 1) * P], ident[:])
                op.then_inc(early_transposed if early else transposed, 1)

            def wait_h(h, stage, t):
                pe.wait_ge(h_ready, tile_index(h, stage, t) + 1)
                pe.wait_ge(h_ready_dve, tile_index(h, stage, t) + 1)

            def first_reduce_mod(f):
                pe.wait_ge(ada_used, NK * (f + 1))
                for v in range(2):
                    for k in range(NK // 2):
                        at = (2 * f + v) * 4 + k
                        start = f * D + v * BLOCK + k * P
                        op = pe.matmul(ps[:, sum_bank(0), at:at + 1], ada_sum[:, start:start + P], ones[:, 0:1],
                                       start=True, stop=True)
                op.then_inc(mod_reduced, 1)

            def reduce_mod(v):
                part = ada_sum[:, v % 2 * D:(v % 2 + 1) * D]
                pe.wait_ge(ada_used, ada_count(v // 2, NK))
                if v > 2:
                    pe.wait_ge(mod_made, v)
                if VECTORS[v][0] == "gate":
                    for i in range(2):
                        op = pe.matmul(ps[:, sum_bank(v) + i, :], ones[:], part[:, i * BLOCK:(i + 1) * BLOCK],
                                       start=True, stop=True)
                else:
                    for k in range(NK):
                        op = pe.matmul(ps[:, sum_bank(v), k:k + 1], part[:, k * P:(k + 1) * P], ones[:, 0:1],
                                       start=True, stop=True)
                op.then_inc(mod_reduced, 1)

            def first_block(banks):
                early, late = range(NK // 2), range(NK // 2, NK)
                for t in range(TB):
                    transpose_tile(0, 0, t)
                pe.wait_ge(early_ready, TB)
                for j in range(3):
                    pe.wait_ge(w_ready, j + 1)
                    project(slot_of(j), 0, banks[j], ks=early)
                    if j == 0:
                        first_reduce_mod(1)
                transpose_tile(0, 0, TB)
                wait_h(0, 0, TB - 1)
                for j in range(3):
                    for t in ((TB + 1,), (TB + 2, TB + 3), ())[j]:
                        transpose_tile(0, 0, t)
                    project(slot_of(j), 0, banks[j], ks=late).then_inc(proj_done, 1)

            def first_chunk(h):
                banks = (4, 6, 0)
                if h == 0:
                    first_block(banks)
                else:
                    wait_h(h, 0, TB - 1)
                    pe.wait_ge(down_added, DOWNS * GROUPS * h + 4 - 3)
                    for j in range(3):
                        if j == 1:
                            pe.wait_ge(down_added, DOWNS * GROUPS * h + 4)
                        pe.wait_ge(w_ready, UNITS * h + j + 1)
                        project(slot_of(j), 0, banks[j], (w_used,) if j == 0 else ()).then_inc(proj_done, 1)
                        if j == 0:
                            for t in range(len(NEXT_A), NT):
                                transpose_tile(h, 0, t)
                            pe.wait_ge(modulated, mod_count(h, 0, NT - 2))
                            pe.wait_ge(modulated_act, mod_count(h, 0, NT - 2))
                wait_h(h, 0, NT - 1)
                for j in range(3):
                    project(slot_of(j), 1, banks[j] + 1, (w_used,) if j > 0 else ()).then_inc(proj_done, 1)

            def stage_b(h, chunk, between=None):
                N = NB * NK * h
                free = (c_copied, m_made, y_made)
                for j in range(3):
                    pe.wait_ge(w_ready, UNITS * h + 3 * chunk + j + 1)
                    for b in range(NB):
                        pe.wait_ge(free[j], N + NB * (chunk - 1) + b + 1)
                        project(slot_of(j), b, (4, 6, 0)[j] + b, (w_used,) if b == 0 else ()).then_inc(proj_done, 1)
                    if j == 0 and between is not None:
                        reduce_mod(between)

            def mixer_step(h, n, halfway=None):
                dh, grp, s = n // 8, n // 4 % 2, n % 4
                slot = slot_of(C0 + 4 * dh + s)
                gone = [y_used] if n > 0 else [w_used]
                if n > 0 and (n - 1) // 4 % 2 == 1:
                    gone.append(w_used)
                if grp == 0:
                    pe.wait_ge(w_ready, UNITS * h + C0 + 4 * dh + s + 1)
                pe.wait_ge(y_split, 16 * h + n + 1)
                for i in range(TB):
                    if i == TB // 2 and halfway is not None:
                        transpose_tile(h, 1, halfway)
                    if s == 0 and n > 0:
                        pe.wait_ge(x1_made, 16 * h + n - TB + i + 1)
                    cut = slice(i * P, (i + 1) * P)
                    op = products(4 + i, [((y_hi[:, n % 2, kk, cut], y_lo[:, n % 2, kk, cut]),
                                           (w_hi[:, slot, kk * BLOCK:(kk + 1) * BLOCK],
                                            w_lo[:, slot, kk * BLOCK:(kk + 1) * BLOCK])) for kk in range(2)],
                                  s == 0, s == 3, gone if i == 0 else ())
                    if s == 3:
                        op.then_inc(mixer_done, 1)

            def up_part(h, q, qe, i, ie, j, b, gone, halfway=None):
                if j == 0 and q >= 2:
                    pe.wait_ge(gated_made, ITEMS * h + q + qe - 1)
                if b == 0:
                    pe.wait_ge(w_ready, UNITS * h + i + ie + 1)
                ks = range(NK)
                if halfway is not None:
                    project(slot_of(i), b, 2 * (q % 2) + j, (w_used,) if gone else (), ks=range(NK // 2))
                    transpose_tile(h, 1, halfway)
                    gone, ks = False, range(NK // 2, NK)
                project(slot_of(i), b, 2 * (q % 2) + j, (w_used,) if gone else (), ks=ks).then_inc(up_done, 1)

            def down(h, g, ge, i, ie, par, next_a=False):
                N = DOWNS * (GROUPS * h + g + ge)
                slots = slot_of(i), slot_of(i + 1)
                pe.wait_ge(w_ready, UNITS * h + i + ie + 2)
                pe.wait_ge(mid_ready, ITEMS * h + 4 * (g + ge) + 4)
                for r in range(DOWNS):
                    t, dh = divmod(r, 2)
                    cut = slice(t * P, (t + 1) * P)
                    pe.wait_ge(down_added, N + r + 1)
                    products(4 + r % 4, [((mid_hi[par][:, j, cut], mid_lo[par][:, j, cut]),
                                          (w_hi[:, slots[j], dh * BLOCK:(dh + 1) * BLOCK],
                                           w_lo[:, slots[j], dh * BLOCK:(dh + 1) * BLOCK])) for j in range(2)],
                             gone=(w_used,) if r == 0 else (),
                             first_done=w_used if r == DOWNS - 1 else None).then_inc(down_done, 1)
                    if next_a and dh == 1 and t in NEXT_A:
                        if t == NEXT_A[0]:
                            pe.wait_ge(gated_made, ITEMS * (h + 1))
                        transpose_tile(h + 1, 0, NEXT_A.index(t))

            pe.wait_ge(const_made, 1)
            pe.wait_ge(vec_loaded, 16 * 6)
            pe.transpose(ps[:, 2, 0:ROWS0], vec_rows[0:ROWS0, 0, :], ident[0:ROWS0, 0:ROWS0])
            pe.transpose(ps[:, 2, ROWS0:ROWS0 + ROWS1], vec_rows[0:ROWS1, 1, :], ident[0:ROWS1, 0:ROWS1]
                         ).then_inc(vec_transposed, 1)
            pe.wait_ge(cols_made, 1)
            for t in range(TB - 2):
                transpose_tile(0, 0, t, early=True)
            first_reduce_mod(0)
            for t in range(TB - 2, TB):
                transpose_tile(0, 0, t, early=True)
            for h in range(HALVES):
                first_chunk(h)
                if h == 0:
                    stage_b(h, 1)
                    reduce_mod(2)
                    stage_b(h, 2, between=3)
                    stage_b(h, 3)
                    reduce_mod(4)
                    stage_b(h, 4, between=5)
                with pe.Fori(5 if h == 0 else 1, NK) as chunk:
                    stage_b(h, chunk)
                for n in range(13):
                    mixer_step(h, n)
                mixer_step(h, 13, halfway=0)
                transpose_tile(h, 1, 1)
                mixer_step(h, 14, halfway=2)
                transpose_tile(h, 1, 3)
                mixer_step(h, 15)
                wait_h(h, 1, TB - 1)
                up_part(h, 0, 0, P0, 0, 0, 0, True)
                transpose_tile(h, 1, TB)
                up_part(h, 0, 0, P0 + 1, 0, 1, 0, False)
                transpose_tile(h, 1, TB + 1)
                transpose_tile(h, 1, TB + 2)
                up_part(h, 1, 0, P0 + 2, 0, 0, 0, False, halfway=TB + 3)
                up_part(h, 1, 0, P0 + 3, 0, 1, 0, False)
                wait_h(h, 1, NT - 1)
                for i in range(4):
                    up_part(h, 2 + i // 2, 0, P0 + i, 0, i % 2, 1, i > 0)
                with pe.Fori(0, (GROUPS - 1) // 2) as g2:
                    for e in range(2):
                        for i in range(4):
                            b = i % 2
                            unit = E0 + 6 * e + 2 * (i // 2)
                            up_part(h, 4 + 4 * e + i, 8 * g2, unit, 12 * g2, 0, b, b == 0)
                            up_part(h, 4 + 4 * e + i, 8 * g2, unit + 1, 12 * g2, 1, b, b == 1)
                        down(h, e, 2 * g2, E0 + 6 * e + 4, 12 * g2, e)
                down(h, GROUPS - 1, 0, L0, 0, 0, h + 1 < HALVES)


_INS = ['x', 'c', 'ln_mix_g', 'ln_ffn_g', 'ada_w', 'ada_b', 'ffn_up', 'ffn_conv', 'ffn_down', 'sc_in', 'sc_conv', 'sc_out']


def kernel(**inputs):
    import numpy as _np
    import concourse.bacc as _bacc
    from concourse import mybir as _mybir
    from concourse.bass_utils import run_bass_kernel_spmd as _run

    nc = _bacc.Bacc("TRN2", target_bir_lowering=False, num_devices=1)
    arrays, args = {}, []
    for name in _INS:
        a = _np.ascontiguousarray(inputs[name])
        arrays[f"in_{name}_dram"] = a
        args.append(nc.dram_tensor(f"in_{name}_dram", a.shape, _mybir.dt.from_np(a.dtype), kind="ExternalInput").ap())
    shape = inputs["x"].shape
    args.append(nc.dram_tensor("out_0_dram", shape, _mybir.dt.float32, kind="ExternalOutput").ap())
    decoder_layer(nc, *args)
    r = _run(nc, [arrays], core_ids=[0])
    return r.results[0]["out_0_dram"]
```
